# Optimizing a Trainium2 kernel written in Bass

```python
import math
import jax
import jax.numpy as jnp
from jax import lax
import numpy as np
import jax, jax.numpy as jnp

D_MODEL = 1024
BATCH = 1
SEQ = 256
DEPTH = 1

HEAD_DIM = 64
A_HEADS = 8
DIL_PATTERNS = ((128, 1), (512, 4), (2048, 16))
DIL_BLOCK = 128
B_HEADS = 8
B_KV_HEADS = 2
B_GROUP = B_HEADS // B_KV_HEADS
CMP_LEN = 32
CMP_STRIDE = 16
CMP_HIDDEN = 128
SEL_BLOCK = 64
SEL_TOPN = 16
SEL_Q_CHUNK = 64
CMP_OVERLAP = (1.0, 2.0, 2.0, 2.0, 1.0)
WIN_LEN = 512
WIN_BLOCK = 128
N_BRANCH = 3
REL_BUCKETS = 32
REL_MAX_DIST = 2048
N_HEADS_TOTAL = A_HEADS + B_HEADS
FFN_HIDDEN = ((-(-8 * D_MODEL // 3)) + 255) // 256 * 256
RMS_EPS = 1e-6
A_WIDTH = A_HEADS * HEAD_DIM
B_WIDTH = B_HEADS * HEAD_DIM
KV_WIDTH = B_KV_HEADS * HEAD_DIM
GATE_WIDTH = B_HEADS * N_BRANCH
IN_SPLITS = (A_WIDTH, A_WIDTH, A_WIDTH, B_WIDTH, KV_WIDTH, KV_WIDTH, KV_WIDTH, KV_WIDTH, KV_WIDTH, KV_WIDTH, GATE_WIDTH)
IN_WIDTH = sum(IN_SPLITS)
SCALE = HEAD_DIM ** -0.5


def rms_norm(x, g):
    xf = x.astype(jnp.float32)
    y = xf * lax.rsqrt(jnp.mean(xf * xf, axis=-1, keepdims=True) + RMS_EPS)
    return (y * g.astype(jnp.float32)).astype(x.dtype)

def t5_bucket(dist):
    max_exact = REL_BUCKETS // 2
    df = jnp.maximum(dist, 1).astype(jnp.float32)
    large = max_exact + (jnp.log(df / max_exact) / math.log(REL_MAX_DIST / max_exact)
                         * (REL_BUCKETS - max_exact)).astype(jnp.int32)
    large = jnp.minimum(large, REL_BUCKETS - 1)
    return jnp.where(dist < max_exact, dist, large)

def masked_softmax(logits, mask):
    logits = jnp.where(mask, logits, -jnp.inf)
    m = jnp.max(logits, axis=-1, keepdims=True)
    m = jnp.where(jnp.isfinite(m), m, 0.0)
    p = jnp.exp(logits - m)
    den = jnp.sum(p, axis=-1, keepdims=True)
    return p / jnp.maximum(den, 1e-30)

def split_columns(t):
    out, start = [], 0
    for w in IN_SPLITS:
        out.append(t[..., start:start + w])
        start += w
    return out

def to_heads(t, n):
    b, s, _ = t.shape
    return t.reshape(b, s, n, HEAD_DIM).transpose(0, 2, 1, 3)

def dilated_attention(q, k, v, table, window, dil):
    b, h, s, dh = q.shape
    steps = window // dil
    unit = dil * DIL_BLOCK
    sp = -(-s // unit) * unit
    length = sp // dil
    nb = length // DIL_BLOCK

    def to_blocks(t):
        t = jnp.pad(t, ((0, 0), (0, 0), (0, sp - s), (0, 0)))
        t = t.reshape(b, h, length, dil, dh).transpose(0, 1, 3, 2, 4)
        return t.reshape(b, h, dil, nb, DIL_BLOCK, dh)

    def with_prev(t):
        prev = jnp.pad(t[:, :, :, :-1], ((0, 0), (0, 0), (0, 0), (1, 0), (0, 0), (0, 0)))
        return jnp.concatenate([prev, t], axis=4)

    qb = to_blocks(q)
    kk = with_prev(to_blocks(k))
    vv = with_prev(to_blocks(v))
    i = jnp.arange(DIL_BLOCK)[:, None]
    j = jnp.arange(2 * DIL_BLOCK)[None, :]
    dist = i + DIL_BLOCK - j
    mask = (dist >= 0) & (dist <= steps)
    first = (jnp.arange(nb)[:, None, None] > 0) | (j[None] >= DIL_BLOCK)
    mask = mask[None] & first
    bias = table[:, t5_bucket(jnp.maximum(dist, 0) * dil)]
    sc = jnp.einsum('bhrnqd,bhrnkd->bhrnqk', qb, kk, preferred_element_type=jnp.float32) * SCALE
    sc = jnp.where(mask, sc + bias[None, :, None, None], -jnp.inf)
    m = jnp.max(sc, axis=-1, keepdims=True)
    p = jnp.exp(sc - m)
    den = jnp.sum(p, axis=-1, keepdims=True)
    o = jnp.einsum('bhrnqk,bhrnkd->bhrnqd', p, vv.astype(jnp.float32)) / den
    lse = (m + jnp.log(den))[..., 0]
    o = o.reshape(b, h, dil, length, dh).transpose(0, 1, 3, 2, 4).reshape(b, h, sp, dh)[:, :, :s]
    lse = lse.reshape(b, h, dil, length).transpose(0, 1, 3, 2).reshape(b, h, sp)[:, :, :s]
    return o, lse

def mixer_dilated(q, k, v, table):
    outs, lses = [], []
    for window, dil in DIL_PATTERNS:
        o, lse = dilated_attention(q, k, v, table, window, dil)
        outs.append(o)
        lses.append(lse)
    w = jax.nn.softmax(jnp.stack(lses, axis=0), axis=0)
    return jnp.sum(w[..., None] * jnp.stack(outs, axis=0), axis=0)

def nsa_compress(kraw, pos, w1, b1, w2):
    b, g, s, dh = kraw.shape
    ch = kraw.reshape(b, g, s // CMP_STRIDE, CMP_STRIDE, dh)
    blk = jnp.concatenate([ch[:, :, :-1], ch[:, :, 1:]], axis=3) + pos
    hid = jax.nn.gelu(jnp.einsum('bgnld,ldh->bgnh', blk, w1) + b1)
    return hid @ w2

def nsa_compressed_branch(q, kc, vc):
    s = q.shape[3]
    nc = kc.shape[2]
    t = jnp.arange(s)
    block_end = jnp.arange(nc) * CMP_STRIDE + CMP_LEN - 1
    mask = block_end[None, :] <= t[:, None]
    sc = jnp.einsum('bgrqd,bgnd->bgrqn', q, kc, preferred_element_type=jnp.float32) * SCALE
    p = masked_softmax(sc, mask)
    o = jnp.einsum('bgrqn,bgnd->bgrqd', p, vc.astype(jnp.float32))
    return o, jnp.sum(p, axis=2)

def block_importance(pc, nb):
    ratio = SEL_BLOCK // CMP_STRIDE
    pp = jnp.pad(pc, ((0, 0), (0, 0), (0, 0), (1, 1)))
    imp = 0.0
    for off, w in zip(range(-1, ratio), CMP_OVERLAP):
        imp = imp + w * pp[..., off + 1: off + 2 + ratio * (nb - 1): ratio]
    return imp

def nsa_selected_branch(q, k, v, imp, table):
    b, g, r, s, dh = q.shape
    nb = s // SEL_BLOCK
    topn = min(SEL_TOPN, nb)
    t = jnp.arange(s)
    cur = (t // SEL_BLOCK)[:, None]
    j = jnp.arange(nb)[None, :]
    forced = (j == 0) | (j == cur) | (j == cur - 1)
    imp = jnp.where(j > cur, -jnp.inf, jnp.where(forced, jnp.inf, imp))
    _, idx = lax.top_k(imp, topn)
    kblk = k.reshape(b, g, nb, SEL_BLOCK * dh)
    vblk = v.reshape(b, g, nb, SEL_BLOCK * dh)
    nch = s // SEL_Q_CHUNK
    qc = q.reshape(b, g, r, nch, SEL_Q_CHUNK, dh).transpose(3, 0, 1, 2, 4, 5)
    ic = idx.reshape(b, g, nch, SEL_Q_CHUNK, topn).transpose(2, 0, 1, 3, 4)
    tab = table.transpose(0, 2, 1)
    b_idx = jnp.arange(b)[:, None, None]
    g_idx3 = jnp.arange(g)[None, :, None]
    g_idx4 = jnp.arange(g)[None, :, None, None]
    nkey = topn * SEL_BLOCK

    def chunk(args):
        qq, ii, c = args
        flat = ii.reshape(b, g, SEL_Q_CHUNK * topn)
        kg = kblk[b_idx, g_idx3, flat].reshape(b, g, SEL_Q_CHUNK, nkey, dh)
        vg = vblk[b_idx, g_idx3, flat].reshape(b, g, SEL_Q_CHUNK, nkey, dh)
        kpos = (ii[..., None] * SEL_BLOCK + jnp.arange(SEL_BLOCK)).reshape(b, g, SEL_Q_CHUNK, nkey)
        tq = c * SEL_Q_CHUNK + jnp.arange(SEL_Q_CHUNK)
        dist = tq[None, None, :, None] - kpos
        bias = tab[g_idx4, t5_bucket(jnp.maximum(dist, 0))].transpose(0, 1, 4, 2, 3)
        sc = jnp.einsum('bgrqd,bgqkd->bgrqk', qq, kg, preferred_element_type=jnp.float32) * SCALE + bias
        p = masked_softmax(sc, (dist >= 0)[:, :, None])
        return jnp.einsum('bgrqk,bgqkd->bgrqd', p, vg.astype(jnp.float32))

    out = lax.map(chunk, (qc, ic, jnp.arange(nch)))
    return out.transpose(1, 2, 3, 0, 4, 5).reshape(b, g, r, s, dh)

def nsa_window_branch(q, k, v, table):
    b, g, r, s, dh = q.shape
    nb = s // WIN_BLOCK
    nw = WIN_LEN // WIN_BLOCK
    qb = q.reshape(b, g, r, nb, WIN_BLOCK, dh)

    def band(t):
        tb = jnp.pad(t.reshape(b, g, nb, WIN_BLOCK, dh), ((0, 0), (0, 0), (nw, 0), (0, 0), (0, 0)))
        return jnp.concatenate([tb[:, :, o:o + nb] for o in range(nw + 1)], axis=3)

    kk, vv = band(k), band(v)
    i = jnp.arange(WIN_BLOCK)[:, None]
    j = jnp.arange((nw + 1) * WIN_BLOCK)[None, :]
    dist = i + nw * WIN_BLOCK - j
    kpos = jnp.arange(nb)[:, None, None] * WIN_BLOCK + j[None] - nw * WIN_BLOCK
    mask = ((dist >= 0) & (dist < WIN_LEN))[None] & (kpos >= 0)
    bias = table[:, :, t5_bucket(jnp.maximum(dist, 0))]
    sc = jnp.einsum('bgrnqd,bgnkd->bgrnqk', qb, kk, preferred_element_type=jnp.float32) * SCALE
    p = masked_softmax(sc + bias[None, :, :, None], mask)
    o = jnp.einsum('bgrnqk,bgnkd->bgrnqd', p, vv.astype(jnp.float32))
    return o.reshape(b, g, r, s, dh)

def first_inputs(seed: int = 0) -> dict:
    key = jax.random.key(seed)
    ks = jax.random.split(key, 18)
    f32 = jnp.float32
    nrm = lambda k, shape, scale: jax.random.normal(k, shape, f32) * scale
    return {
        "x": nrm(ks[0], (BATCH, SEQ, D_MODEL), 1.0),
        "norm1_g": 1.0 + nrm(ks[1], (DEPTH, D_MODEL), 0.02),
        "w_in": nrm(ks[2], (DEPTH, D_MODEL, IN_WIDTH), D_MODEL ** -0.5),
        "rel_bias": nrm(ks[3], (REL_BUCKETS, N_HEADS_TOTAL), 0.1),
        "cmp_pos": nrm(ks[4], (DEPTH, CMP_LEN, HEAD_DIM), 0.2),
        "cmp_k_w1": nrm(ks[5], (DEPTH, CMP_LEN, HEAD_DIM, CMP_HIDDEN), (CMP_LEN * HEAD_DIM) ** -0.5),
        "cmp_k_b1": nrm(ks[6], (DEPTH, CMP_HIDDEN), 0.02),
        "cmp_k_w2": nrm(ks[7], (DEPTH, CMP_HIDDEN, HEAD_DIM), CMP_HIDDEN ** -0.5),
        "cmp_v_w1": nrm(ks[8], (DEPTH, CMP_LEN, HEAD_DIM, CMP_HIDDEN), (CMP_LEN * HEAD_DIM) ** -0.5),
        "cmp_v_b1": nrm(ks[9], (DEPTH, CMP_HIDDEN), 0.02),
        "cmp_v_w2": nrm(ks[10], (DEPTH, CMP_HIDDEN, HEAD_DIM), CMP_HIDDEN ** -0.5),
        "w_out": nrm(ks[11], (DEPTH, A_WIDTH + B_WIDTH, D_MODEL), (A_WIDTH + B_WIDTH) ** -0.5),
        "norm2_g": 1.0 + nrm(ks[12], (DEPTH, D_MODEL), 0.02),
        "w_gate": nrm(ks[13], (DEPTH, D_MODEL, FFN_HIDDEN), D_MODEL ** -0.5),
        "w_up": nrm(ks[14], (DEPTH, D_MODEL, FFN_HIDDEN), D_MODEL ** -0.5),
        "w_down": nrm(ks[15], (DEPTH, FFN_HIDDEN, D_MODEL), FFN_HIDDEN ** -0.5),
        "norm_f_g": 1.0 + nrm(ks[16], (D_MODEL,), 0.02),
    }

def first_block(x, norm1_g, w_in, rel_bias, cmp_pos, cmp_k_w1, cmp_k_b1, cmp_k_w2,
              cmp_v_w1, cmp_v_b1, cmp_v_w2, w_out, norm2_g, w_gate, w_up, w_down, norm_f_g):
    b, s, _ = x.shape
    tab_a = rel_bias[:, :A_HEADS].T
    tab_b = rel_bias[:, A_HEADS:].T.reshape(B_KV_HEADS, B_GROUP, REL_BUCKETS)
    h = x
    for layer in range(DEPTH):
        xn = rms_norm(h, norm1_g[layer])
        aq, ak, av, bq, kc, vc, ksl, vsl, kw, vw, gl = split_columns(xn @ w_in[layer])
        o_a = mixer_dilated(to_heads(aq, A_HEADS), to_heads(ak, A_HEADS), to_heads(av, A_HEADS), tab_a)
        q_b = to_heads(bq, B_HEADS).reshape(b, B_KV_HEADS, B_GROUP, s, HEAD_DIM)
        k_cmp = nsa_compress(to_heads(kc, B_KV_HEADS), cmp_pos[layer], cmp_k_w1[layer], cmp_k_b1[layer], cmp_k_w2[layer])
        v_cmp = nsa_compress(to_heads(vc, B_KV_HEADS), cmp_pos[layer], cmp_v_w1[layer], cmp_v_b1[layer], cmp_v_w2[layer])
        o_cmp, p_cmp = nsa_compressed_branch(q_b, k_cmp, v_cmp)
        imp = block_importance(p_cmp, s // SEL_BLOCK)
        o_slc = nsa_selected_branch(q_b, to_heads(ksl, B_KV_HEADS), to_heads(vsl, B_KV_HEADS), imp, tab_b)
        o_win = nsa_window_branch(q_b, to_heads(kw, B_KV_HEADS), to_heads(vw, B_KV_HEADS), tab_b)
        gate = jax.nn.sigmoid(gl.astype(jnp.float32)).reshape(b, s, B_KV_HEADS, B_GROUP, N_BRANCH).transpose(0, 2, 3, 1, 4)
        o_b = gate[..., 0:1] * o_cmp + gate[..., 1:2] * o_slc + gate[..., 2:3] * o_win
        mix = jnp.concatenate([
            o_a.transpose(0, 2, 1, 3).reshape(b, s, A_WIDTH),
            o_b.reshape(b, B_HEADS, s, HEAD_DIM).transpose(0, 2, 1, 3).reshape(b, s, B_WIDTH),
        ], axis=-1).astype(h.dtype)
        h = h + mix @ w_out[layer]
        hn = rms_norm(h, norm2_g[layer])
        h = h + (jax.nn.silu(hn @ w_gate[layer]) * (hn @ w_up[layer])) @ w_down[layer]
    return rms_norm(h, norm_f_g)


DEPTH_2 = 2

GRID_W = 64
CTX_LEN = 256

ATT_HEADS = 8
ATT_HEAD_DIM = 64
ATT_QK_DIM = ATT_HEADS * 2 * ATT_HEAD_DIM
ATT_V_DIM = ATT_HEADS * 2 * ATT_HEAD_DIM
Q_BLOCK = 128
ROPE_BASE = 10000.0
ROPE_PAIRS = ATT_HEAD_DIM // 4

SSD_D_INNER = 2 * D_MODEL
SSD_HEAD_DIM = 64
SSD_HEADS = SSD_D_INNER // SSD_HEAD_DIM
SSD_GROUPS = 8
SSD_STATE = 128
SSD_CONV = 5
SSD_CHUNK = 128
SSD_CONV_DIM = SSD_D_INNER + 2 * SSD_GROUPS * SSD_STATE

D_FF = 4 * D_MODEL

N_BRANCH_2 = 2
N_MOD = 6
IN_DIM = 2 * ATT_QK_DIM + ATT_V_DIM + SSD_D_INNER + SSD_CONV_DIM + 2 * SSD_HEADS + N_BRANCH_2 * D_MODEL


def rmsnorm(x, g, eps=1e-6):
    xf = x.astype(jnp.float32)
    y = xf * lax.rsqrt(jnp.mean(xf * xf, axis=-1, keepdims=True) + eps)
    return (y * g.astype(jnp.float32)).astype(x.dtype)

def modulate(x, g, shift, scale):
    return rmsnorm(x, g) * (1 + scale) + shift

def in_proj_split(t):
    sizes = (ATT_QK_DIM, ATT_QK_DIM, ATT_V_DIM, SSD_D_INNER, SSD_CONV_DIM,
             SSD_HEADS, SSD_HEADS, D_MODEL, D_MODEL)
    idx, acc = [], 0
    for s in sizes[:-1]:
        acc += s
        idx.append(acc)
    return jnp.split(t, idx, axis=-1)

def axial_rope(n_tok):
    rows = n_tok // GRID_W
    row = jnp.broadcast_to(jnp.arange(rows)[:, None], (rows, GRID_W)).reshape(-1).astype(jnp.float32)
    col = jnp.broadcast_to(jnp.arange(GRID_W)[None, :], (rows, GRID_W)).reshape(-1).astype(jnp.float32)
    inv = jnp.float32(ROPE_BASE) ** (-jnp.arange(ROPE_PAIRS, dtype=jnp.float32) / ROPE_PAIRS)
    ang = jnp.concatenate([row[:, None] * inv, col[:, None] * inv], axis=-1)
    return jnp.cos(ang), jnp.sin(ang)

def apply_rope(x, cos, sin):
    half = x.shape[-1] // 2
    x1 = x[..., :half].astype(jnp.float32)
    x2 = x[..., half:].astype(jnp.float32)
    c = cos[:, None, None, :]
    s = sin[:, None, None, :]
    return jnp.concatenate([x1 * c - x2 * s, x1 * s + x2 * c], axis=-1).astype(x.dtype)

def diff_attend(q, k, v, lam):
    s = jnp.einsum('bqhcd,bkhcd->bchqk', q, k).astype(jnp.float32) * (ATT_HEAD_DIM ** -0.5)
    p = jax.nn.softmax(s, axis=-1)
    a = p[:, 0] - lam * p[:, 1]
    return jnp.einsum('bhqk,bkhe->bqhe', a.astype(v.dtype), v)

def diff_attention(q_l, k_l, v_l, q_c, k_c, v_c, lam, lam_init, subln_g, with_ctx_out):
    b, n, h = q_l.shape[:3]
    k_all = jnp.concatenate([k_l, k_c], axis=1)
    v_all = jnp.concatenate([v_l, v_c], axis=1)
    nb = n // Q_BLOCK
    qb = jnp.moveaxis(q_l.reshape(b, nb, Q_BLOCK, h, 2, ATT_HEAD_DIM), 1, 0)
    o_l = lax.map(lambda qq: diff_attend(qq, k_all, v_all, lam), qb)
    o_l = jnp.moveaxis(o_l, 0, 1).reshape(b, n, h, 2 * ATT_HEAD_DIM)

    def post(o):
        return (rmsnorm(o, subln_g) * (1.0 - lam_init)).reshape(o.shape[0], o.shape[1], ATT_V_DIM)

    o_c = post(diff_attend(q_c, k_c, v_c, lam)) if with_ctx_out else None
    return post(o_l), o_c

def dwconv_silu(x, w, bias):
    kw = w.shape[0]
    y = lax.conv_general_dilated(x, w.astype(x.dtype)[:, None, :], window_strides=(1,),
                                 padding=[(kw // 2, kw // 2)],
                                 dimension_numbers=('NWC', 'WIO', 'NWC'),
                                 feature_group_count=x.shape[-1])
    return jax.nn.silu(y + bias)

def ssd_chunked(x, dt, a, bm, cm, h0, need_y):
    f32 = jnp.float32
    out_dtype = x.dtype
    b, n, h, p = x.shape
    g, ns = bm.shape[2], bm.shape[3]
    r = h // g
    nc = n // SSD_CHUNK
    dt = dt.astype(f32)
    xc = (x.astype(f32) * dt[..., None]).reshape(b, nc, SSD_CHUNK, g, r, p)
    cs = jnp.cumsum((dt * a.astype(f32)).reshape(b, nc, SSD_CHUNK, g, r), axis=2)
    bc = bm.astype(f32).reshape(b, nc, SSD_CHUNK, g, ns)
    cc = cm.astype(f32).reshape(b, nc, SSD_CHUNK, g, ns)
    decay_to_end = jnp.exp(cs[:, :, -1:] - cs)
    chunk_states = jnp.einsum('bclgn,bclgr,bclgrp->bcgrpn', bc, decay_to_end, xc)
    chunk_decay = jnp.exp(cs[:, :, -1])

    def step(hc, inp):
        st, dec = inp
        return hc * dec[..., None, None] + st, hc

    h_last, h_in = lax.scan(step, h0.astype(f32),
                            (jnp.moveaxis(chunk_states, 1, 0), jnp.moveaxis(chunk_decay, 1, 0)))
    if not need_y:
        return None, h_last
    h_in = jnp.moveaxis(h_in, 0, 1)
    seg = cs[:, :, :, None] - cs[:, :, None, :]
    lower = jnp.tril(jnp.ones((SSD_CHUNK, SSD_CHUNK), dtype=bool))[:, :, None, None]
    lmat = jnp.exp(jnp.where(lower, seg, -jnp.inf))
    cb = jnp.einsum('bclgn,bcsgn->bclsg', cc, bc)
    y = (jnp.einsum('bclsg,bclsgr,bcsgrp->bclgrp', cb, lmat, xc)
         + jnp.einsum('bclgn,bcgrpn,bclgr->bclgrp', cc, h_in, jnp.exp(cs)))
    return y.reshape(b, n, h, p).astype(out_dtype), h_last

def ssd_inputs(xbc_raw, dtf_raw, dtb_raw, conv_w, conv_b, dt_bias_f, dt_bias_b):
    xbc = dwconv_silu(xbc_raw, conv_w, conv_b)
    xs, bm, cm = jnp.split(xbc, [SSD_D_INNER, SSD_D_INNER + SSD_GROUPS * SSD_STATE], axis=-1)
    b, n = xs.shape[:2]
    xs = xs.reshape(b, n, SSD_HEADS, SSD_HEAD_DIM)
    bm = bm.reshape(b, n, SSD_GROUPS, SSD_STATE)
    cm = cm.reshape(b, n, SSD_GROUPS, SSD_STATE)
    dt_f = jax.nn.softplus((dtf_raw + dt_bias_f).astype(jnp.float32))
    dt_b = jax.nn.softplus((dtb_raw + dt_bias_b).astype(jnp.float32))
    return xs, bm, cm, dt_f, dt_b

def ssd_output(yf, yb, xs, z, ssd_d, ssd_norm_g, w_ssd_o):
    b, n = xs.shape[:2]
    y = (yf + yb + ssd_d[:, None] * xs).reshape(b, n, SSD_D_INNER)
    return rmsnorm(y * jax.nn.silu(z), ssd_norm_g) @ w_ssd_o

def hybrid_mixer(h_l, h_c, cos, sin, w_in, conv_w, conv_b, dt_bias_f, dt_bias_b, a_log_f, a_log_b,
                 ssd_d, ssd_norm_g, lam, lam_init, subln_g, w_attn_o, w_ssd_o, w_out, with_ctx_out):
    ql, kl, vl, zl, xbcl, dtfl, dtbl, gal, gsl = in_proj_split(h_l @ w_in)
    qc, kc, vc, zc, xbcc, dtfc, dtbc, gac, gsc = in_proj_split(h_c @ w_in)

    def qk(t):
        return t.reshape(t.shape[0], t.shape[1], ATT_HEADS, 2, ATT_HEAD_DIM)

    def vv(t):
        return t.reshape(t.shape[0], t.shape[1], ATT_HEADS, 2 * ATT_HEAD_DIM)

    att_l, att_c = diff_attention(apply_rope(qk(ql), cos, sin), apply_rope(qk(kl), cos, sin), vv(vl),
                                  qk(qc), qk(kc), vv(vc), lam, lam_init, subln_g, with_ctx_out)

    a_f = -jnp.exp(a_log_f.astype(jnp.float32))
    a_b = -jnp.exp(a_log_b.astype(jnp.float32))
    rev = lambda t: jnp.flip(t, axis=1)
    xs_c, bm_c, cm_c, dtf_c, dtb_c = ssd_inputs(xbcc, dtfc, dtbc, conv_w, conv_b, dt_bias_f, dt_bias_b)
    xs_l, bm_l, cm_l, dtf_l, dtb_l = ssd_inputs(xbcl, dtfl, dtbl, conv_w, conv_b, dt_bias_f, dt_bias_b)
    b = h_l.shape[0]
    h0 = jnp.zeros((b, SSD_GROUPS, SSD_HEADS // SSD_GROUPS, SSD_HEAD_DIM, SSD_STATE), jnp.float32)
    yc_f, st_f = ssd_chunked(xs_c, dtf_c, a_f, bm_c, cm_c, h0, with_ctx_out)
    yc_b, st_b = ssd_chunked(rev(xs_c), rev(dtb_c), a_b, rev(bm_c), rev(cm_c), h0, with_ctx_out)
    yl_f, _ = ssd_chunked(xs_l, dtf_l, a_f, bm_l, cm_l, st_f, True)
    yl_b, _ = ssd_chunked(rev(xs_l), rev(dtb_l), a_b, rev(bm_l), rev(cm_l), st_b, True)
    ssd_l = ssd_output(yl_f, rev(yl_b), xs_l, zl, ssd_d, ssd_norm_g, w_ssd_o)

    def merge(att, ssd, ga, gs):
        return (jax.nn.sigmoid(ga) * (att @ w_attn_o) + jax.nn.sigmoid(gs) * ssd) @ w_out

    o_l = merge(att_l, ssd_l, gal, gsl)
    o_c = None
    if with_ctx_out:
        ssd_c = ssd_output(yc_f, rev(yc_b), xs_c, zc, ssd_d, ssd_norm_g, w_ssd_o)
        o_c = merge(att_c, ssd_c, gac, gsc)
    return o_l, o_c

def sq_relu_mlp(h, w1, w2):
    return jnp.square(jax.nn.relu(h @ w1)) @ w2

def second_inputs(seed: int = 0) -> dict:
    key = jax.random.key(seed)
    ks = jax.random.split(key, 32)
    f32 = jnp.float32

    def nrm(k, shape, scale):
        return jax.random.normal(k, shape, f32) * scale

    def gain(k, shape):
        return 1.0 + 0.05 * jax.random.normal(k, shape, f32)

    dt = jnp.exp(jax.random.uniform(ks[10], (DEPTH_2, 2, SSD_HEADS), f32,
                                    math.log(1e-3), math.log(1e-1)))
    dt_bias = dt + jnp.log(-jnp.expm1(-dt))
    a_log = jnp.log(jax.random.uniform(ks[11], (DEPTH_2, 2, SSD_HEADS), f32, 1.0, 16.0))
    return {
        'x': nrm(ks[0], (BATCH, SEQ, D_MODEL), 1.0),
        'c': nrm(ks[1], (BATCH, D_MODEL), 1.0),
        'ctx': nrm(ks[2], (BATCH, CTX_LEN, D_MODEL), 1.0),
        'c_ctx': nrm(ks[3], (D_MODEL,), 1.0),
        'ada_w': nrm(ks[4], (DEPTH_2, D_MODEL, N_MOD * D_MODEL), 0.5 * D_MODEL ** -0.5),
        'ada_b': nrm(ks[5], (DEPTH_2, N_MOD * D_MODEL), 0.02),
        'norm_mix_g': gain(ks[6], (DEPTH_2, D_MODEL)),
        'w_in': nrm(ks[7], (DEPTH_2, D_MODEL, IN_DIM), D_MODEL ** -0.5),
        'conv_w': nrm(ks[8], (DEPTH_2, SSD_CONV, SSD_CONV_DIM), SSD_CONV ** -0.5),
        'conv_b': nrm(ks[9], (DEPTH_2, SSD_CONV_DIM), 0.02),
        'dt_bias_f': dt_bias[:, 0],
        'dt_bias_b': dt_bias[:, 1],
        'a_log_f': a_log[:, 0],
        'a_log_b': a_log[:, 1],
        'ssd_d': gain(ks[12], (DEPTH_2, SSD_HEADS)),
        'ssd_norm_g': gain(ks[13], (DEPTH_2, SSD_D_INNER)),
        'lambda_q1': nrm(ks[14], (DEPTH_2, ATT_HEAD_DIM), 0.1),
        'lambda_k1': nrm(ks[15], (DEPTH_2, ATT_HEAD_DIM), 0.1),
        'lambda_q2': nrm(ks[16], (DEPTH_2, ATT_HEAD_DIM), 0.1),
        'lambda_k2': nrm(ks[17], (DEPTH_2, ATT_HEAD_DIM), 0.1),
        'attn_subln_g': gain(ks[18], (DEPTH_2, 2 * ATT_HEAD_DIM)),
        'w_attn_o': nrm(ks[19], (DEPTH_2, ATT_V_DIM, D_MODEL), ATT_V_DIM ** -0.5),
        'w_ssd_o': nrm(ks[20], (DEPTH_2, SSD_D_INNER, D_MODEL), SSD_D_INNER ** -0.5),
        'w_out': nrm(ks[21], (DEPTH_2, D_MODEL, D_MODEL), D_MODEL ** -0.5),
        'norm_mlp_g': gain(ks[22], (DEPTH_2, D_MODEL)),
        'w_mlp1': nrm(ks[23], (DEPTH_2, D_MODEL, D_FF), D_MODEL ** -0.5),
        'w_mlp2': nrm(ks[24], (DEPTH_2, D_FF, D_MODEL), D_FF ** -0.5),
        'final_norm_g': gain(ks[25], (D_MODEL,)),
    }

def second_block(x, c, ctx, c_ctx, ada_w, ada_b, norm_mix_g, w_in, conv_w, conv_b, dt_bias_f, dt_bias_b,
              a_log_f, a_log_b, ssd_d, ssd_norm_g, lambda_q1, lambda_k1, lambda_q2, lambda_k2,
              attn_subln_g, w_attn_o, w_ssd_o, w_out, norm_mlp_g, w_mlp1, w_mlp2, final_norm_g):
    n_lat = x.shape[1]
    cos, sin = axial_rope(n_lat)
    c_act = jax.nn.silu(c)
    cc_act = jax.nn.silu(c_ctx)
    xl, xc = x, ctx
    for l in range(DEPTH_2):
        last = l == DEPTH_2 - 1
        mod_l = [m[:, None, :] for m in jnp.split(c_act @ ada_w[l] + ada_b[l], N_MOD, axis=-1)]
        mod_c = jnp.split(cc_act @ ada_w[l] + ada_b[l], N_MOD, axis=-1)
        lam_init = 0.8 - 0.6 * math.exp(-0.3 * l)
        lam = (jnp.exp(jnp.sum(lambda_q1[l].astype(jnp.float32) * lambda_k1[l].astype(jnp.float32)))
               - jnp.exp(jnp.sum(lambda_q2[l].astype(jnp.float32) * lambda_k2[l].astype(jnp.float32)))
               + lam_init)
        h_l = modulate(xl, norm_mix_g[l], mod_l[0], mod_l[1])
        h_c = modulate(xc, norm_mix_g[l], mod_c[0], mod_c[1])
        o_l, o_c = hybrid_mixer(h_l, h_c, cos, sin, w_in[l], conv_w[l], conv_b[l], dt_bias_f[l], dt_bias_b[l],
                                a_log_f[l], a_log_b[l], ssd_d[l], ssd_norm_g[l], lam, lam_init,
                                attn_subln_g[l], w_attn_o[l], w_ssd_o[l], w_out[l], not last)
        xl = xl + mod_l[2] * o_l
        xl = xl + mod_l[5] * sq_relu_mlp(modulate(xl, norm_mlp_g[l], mod_l[3], mod_l[4]), w_mlp1[l], w_mlp2[l])
        if not last:
            xc = xc + mod_c[2] * o_c
            xc = xc + mod_c[5] * sq_relu_mlp(modulate(xc, norm_mlp_g[l], mod_c[3], mod_c[4]), w_mlp1[l], w_mlp2[l])
    return rmsnorm(xl, final_norm_g)


def setup_inputs(seed=0):
    out = dict(first_inputs(seed))
    for name, value in second_inputs(seed + 1).items():
        if name != "x":
            out[name + "_2"] = value
    return out


def reference(
    x, norm1_g, w_in, rel_bias, cmp_pos, cmp_k_w1, cmp_k_b1, cmp_k_w2, cmp_v_w1, cmp_v_b1,
    cmp_v_w2, w_out, norm2_g, w_gate, w_up, w_down, norm_f_g, c_2, ctx_2, c_ctx_2, ada_w_2,
    ada_b_2, norm_mix_g_2, w_in_2, conv_w_2, conv_b_2, dt_bias_f_2, dt_bias_b_2, a_log_f_2,
    a_log_b_2, ssd_d_2, ssd_norm_g_2, lambda_q1_2, lambda_k1_2, lambda_q2_2, lambda_k2_2,
    attn_subln_g_2, w_attn_o_2, w_ssd_o_2, w_out_2, norm_mlp_g_2, w_mlp1_2, w_mlp2_2,
    final_norm_g_2,
):
    x = first_block(
        x, norm1_g, w_in, rel_bias, cmp_pos, cmp_k_w1, cmp_k_b1, cmp_k_w2, cmp_v_w1, cmp_v_b1,
        cmp_v_w2, w_out, norm2_g, w_gate, w_up, w_down, norm_f_g,
    )
    return second_block(
        x, c_2, ctx_2, c_ctx_2, ada_w_2, ada_b_2, norm_mix_g_2, w_in_2, conv_w_2, conv_b_2,
        dt_bias_f_2, dt_bias_b_2, a_log_f_2, a_log_b_2, ssd_d_2, ssd_norm_g_2, lambda_q1_2,
        lambda_k1_2, lambda_q2_2, lambda_k2_2, attn_subln_g_2, w_attn_o_2, w_ssd_o_2, w_out_2,
        norm_mlp_g_2, w_mlp1_2, w_mlp2_2, final_norm_g_2,
    )


_drawn_inputs = setup_inputs


def setup_inputs(seed=0):
    import zlib

    import numpy as np

    out = dict(_drawn_inputs(seed))
    spreads = {}
    factors = {'norm1_g': 6.628,
     'rel_bias': 3.438,
     'cmp_k_b1': 8.0,
     'cmp_v_b1': 8.0,
     'norm2_g': 3.781,
     'norm_f_g': 2.703,
     'norm_mix_g_2': 3.022,
     'conv_b_2': 8.0,
     'ssd_d_2': 8.0,
     'ssd_norm_g_2': 5.019,
     'lambda_q1_2': 3.237,
     'lambda_k1_2': 8.0,
     'lambda_q2_2': 6.235,
     'lambda_k2_2': 7.09,
     'attn_subln_g_2': 6.591}
    for name, (base, spread) in spreads.items():
        noise = np.random.default_rng([zlib.crc32(name.encode()), seed]).standard_normal(out[name].shape)
        drawn = base * np.exp(spread * noise) if base else spread * noise
        out[name] = jnp.asarray(drawn.astype(out[name].dtype))
    for name, factor in factors.items():
        out[name] = (out[name] * factor).astype(out[name].dtype)
    return out
```

```python
import math
from contextlib import ExitStack

import numpy as np

import concourse.bass as bass
from concourse import mybir

S = 256
T = 512
D = 1024
P = 128
KC = D // P
HD = 64
NEG = -1.0e30
EPS = 1e-6
FFN1 = 2816
FC1 = FFN1 // P
FFC = 4 * D // P
NG = 8
DI = 2048
QKV = 1024
SSD_Z = 3 * QKV
SSD_X = SSD_Z + DI
SSD_B = SSD_X + DI
SSD_C = SSD_B + 1024
SSD_DT = SSD_C + 1024
GATE_A = SSD_DT + 64
GATE_S = GATE_A + D
SLOTS = 10
LINE = 383

C_ID, C_UP, C_LO, C_ONE, C_PERM = 0, 128, 256, 384, 512
C_COS, C_SIN, C_CMP = 640, 896, 1152
C_END = 1182

PARAM_ROWS = {
    "norm1_g": (0, 0), "norm2_g": (0, 8), "norm_f_g": (0, 16), "mix0": (0, 24), "mix1": (0, 32),
    "mlp0": (0, 40), "mlp1": (0, 48), "final": (0, 56), "ssdg0": (0, 64), "ssdg1": (0, 80),
    "c": (0, 96), "cctx": (0, 104), "subln0": (0, 112), "subln1": (0, 113), "kb1": (0, 114), "vb1": (0, 115),
    "ada0": (1, 0), "ada1": (1, 48),
    "cwA0": (2, 0), "cwB0": (3, 0), "cb0": (3, 64), "cwA1": (4, 0), "cwB1": (5, 0), "cb1": (5, 64),
}
PARAM_SIZE = [116, 96, 96, 96, 96, 96]

PHASES = ["setup", "bias", "norm1", "A", "B", "wout1", "norm2", "ffn1", "down1", "normf1"]
for _l in range(2):
    PHASES += [f"{n}{_l}" for n in ("ada", "mixnorm", "dt", "ssd", "att", "merge", "wout2", "mlpnorm", "f1", "f2")]
PHASES += ["normend", "out"]
NORMS = ["norm1", "norm2", "normf1", "mixnorm0", "mlpnorm0", "mixnorm1", "mlpnorm1", "normend"]

ADA = {
    "A": (0, [3, 4, 5, 6, 7, 8], 0, 2), "wout1": (0, [4, 5, 6, 7, 8, 9], 24, 0), "down1": (0, [4, 5, 6], 36, 0),
    "ssd0": (1, [5, 6, 7, 8], 0, 4), "att0": (1, [8, 9], 32, 2),
}

FWD = [2, 3, 0, 1]
BWD = [3, 2, 1, 0]


def t5_buckets(dist):
    large = 16 + (np.log(np.maximum(dist, 1).astype(np.float32) / np.float32(16))
                  / math.log(2048 / 16) * 16).astype(np.int32)
    return np.where(dist < 16, dist, np.minimum(large, 31))


def constants():
    c = np.zeros((P, C_END), np.float32)
    p = np.arange(P)
    c[:, C_ID:C_ID + P] = np.eye(P)
    c[:, C_UP:C_UP + P] = p[:, None] <= p[None]
    c[:, C_LO:C_LO + P] = p[:, None] >= p[None]
    c[:, C_ONE:C_ONE + P] = 1.0
    for o in range(0, P, 64):
        for r in range(32):
            c[o + 32 + r, C_PERM + o + r] = -1.0
            c[o + r, C_PERM + o + 32 + r] = 1.0
    inv = np.float32(10000.0) ** (-np.arange(16, dtype=np.float32) / 16)
    t = np.arange(S)
    ang = np.concatenate([(t // 64).astype(np.float32)[:, None] * inv, (t % 64).astype(np.float32)[:, None] * inv], 1)
    c[:, C_COS:C_COS + S] = np.cos(ang).T[p % 32]
    c[:, C_SIN:C_SIN + S] = np.sin(ang).T[p % 32]
    for qt in range(2):
        ends = np.arange(15) * 16 + 31
        c[:, C_CMP + 15 * qt:C_CMP + 15 * qt + 15] = np.where(ends[None] <= (p + 128 * qt)[:, None], 0.0, NEG)
    dist = np.arange(LINE) - 127
    hot = (t5_buckets(np.maximum(dist, 0))[None] == np.arange(32)[:, None]).astype(np.float32)
    times = (dist <= 128).astype(int) + (dist % 4 == 0) + (dist % 16 == 0)
    dilated = np.where((dist >= 0) & (times > 0), np.log(np.maximum(times, 1)), NEG)
    causal = np.where(dist >= 0, 0.0, NEG)
    lines = np.concatenate([np.tile(dilated, (8, 1)), np.tile(causal, (8, 1))]).astype(np.float32)
    return {"const": c, "onehot": hot, "lines": lines}


def chunked(w):
    return w.rearrange("(c p) n -> p c n", p=P)


def weight_loads(a):
    w1 = chunked(a["w_in"][0])
    wo = chunked(a["w_out"][0])
    wg, wu, wd = chunked(a["w_gate"][0]), chunked(a["w_up"][0]), chunked(a["w_down"][0])

    def col(w, base, step=P, n=P, k0=0, k1=KC):
        return lambda i: [((0, k1 - k0, 0, n), w[:, k0:k1, bass.ds(base + i * step, n)])]

    def twice(w, base):
        return lambda i: [((0, KC, 64 * d, 64), w[:, :, bass.ds(base + i * 64, 64)]) for d in range(2)]

    def pair(w, b0, b1):
        return lambda i: [((0, KC, 0, 64), w[:, :, bass.ds(b0 + i * 64, 64)]),
                          ((0, KC, 64, 64), w[:, :, bass.ds(b1 + i * 64, 64)])]

    loads = {
        "A": (4, [(0, col(w1, 0)), (1, col(w1, 512)), (2, col(w1, 1024))]),
        "B": (2, [(3, lambda i: [((0, KC, 0, 24), w1[:, :, 2816:2840])]),
                  (4, col(w1, 1536, 256)), (5, col(w1, 1664, 256)),
                  (6, pair(w1, 2048, 2176)), (7, twice(w1, 2304)), (8, twice(w1, 2560)),
                  (9, pair(w1, 2432, 2688))]),
        "wout1": (2, [(t, col(wo, t * P, 4 * P)) for t in range(4)]),
        "ffn1": (FC1 // 2, [(4, col(wg, 0, 256)), (5, col(wu, 0, 256)), (6, col(wg, P, 256)), (7, col(wu, P, 256))]),
        "down1": (4, [(s, col(wd, P * (n // 3), 256, P, 8 * (n % 3), min(8 * (n % 3) + 8, FC1)))
                      for n, s in enumerate([8, 9, 0, 1, 2, 3])]),
    }
    beside = {}
    for l in range(2):
        wi, ada = chunked(a["w_in_2"][l]), chunked(a["ada_w_2"][l])
        ao, so, wo2 = chunked(a["w_attn_o_2"][l]), chunked(a["w_ssd_o_2"][l]), chunked(a["w_out_2"][l])
        m1, m2 = chunked(a["w_mlp1_2"][l]), chunked(a["w_mlp2_2"][l])
        for ph, (layer, slots, first, _) in ADA.items():
            if layer == l:
                beside[ph] = [(s, col(ada, (first + t) * P, len(slots) * P)) for t, s in enumerate(slots)]
        loads[f"dt{l}"] = (1, [(8, col(wi, SSD_DT, 64, 64))])
        loads[f"ssd{l}"] = (NG, [(9, col(wi, SSD_X, 256)), (0, col(wi, SSD_X + P, 256)), (1, col(wi, SSD_B)),
                                 (2, col(wi, SSD_C)), (3, col(wi, SSD_Z, 256)), (4, col(wi, SSD_Z + P, 256))])
        loads[f"att{l}"] = (8, [(7, col(wi, 2 * QKV)), (5, col(wi, 0)), (6, col(wi, QKV))])
        loads[f"merge{l}"] = (8, [(8, col(wi, GATE_A)), (9, col(wi, GATE_S)), (0, col(ao, 0)),
                                  (1, col(so, 0)), (2, col(so, 0, P, P, 8, 16))])
        loads[f"wout2{l}"] = (2, [(3 + t, col(wo2, t * P, 4 * P)) for t in range(4)])
        loads[f"f1{l}"] = (8, [(s, col(m1, t * P, 4 * P)) for t, s in enumerate([7, 8, 9, 0])])
        loads[f"f2{l}"] = (4, [(1 + n, col(m2, P * (n // 4), 256, P, 8 * (n % 4), 8 * (n % 4) + 8)) for n in range(8)])
    for ph, tiles in beside.items():
        loads[ph][1].extend(tiles)
    return loads


def softmax_units_a():
    units = []
    for h in range(2):
        for qt in range(2):
            units.append(dict(part=64 * h, q=qt * P, k0=0, nk=P * (qt + 1), head=h, qt=qt,
                              out=(64 * h, qt * P), first=True, last=True))
    return units


def softmax_units_b():
    units = []
    for r in range(4):
        for qt in range(2):
            for br in range(3):
                units.append(dict(part=64 * (r % 2), q=qt * P, k0=0, nk=15 if br == 0 else P * (qt + 1), head=r, qt=qt,
                                  branch=br, out=(64 * (r % 2), (r // 2) * S + qt * P), first=br == 0, last=br == 2))
    return units


def softmax_units_diff(last_layer):
    units = []
    for qt in range(2 if last_layer else 4):
        for c in range(2):
            units.append(dict(part=64 * c, q=qt * P, k0=0 if qt < 2 else S, nk=T if qt < 2 else S, qt=qt, comp=c,
                              out=(0, qt * P), first=c == 0, last=c == 1))
    return units


def build(nc, a, out):
    fp32 = mybir.dt.float32
    ALU = mybir.AluOpType
    ACT = mybir.ActivationFunctionType
    AX = mybir.AxisListType

    loads = weight_loads(a)
    phase_no = {n: k for k, n in enumerate(PHASES)}
    uses, fills, before, per_fill = [0] * SLOTS, [0] * SLOTS, {}, {}
    for ph in PHASES:
        if ph in loads:
            times, tiles = loads[ph]
            for s, src in tiles:
                before[ph, s] = (uses[s], fills[s])
                per_fill[ph, s] = 16 * len(src(0))
                uses[s] += times
                fills[s] += times * per_fill[ph, s]

    cs_dram = nc.dram_tensor("cs_rows", [64, T], fp32, kind="Internal")
    line_dram = nc.dram_tensor("bias_lines", [16, LINE], fp32, kind="Internal")

    ctx = ExitStack()
    with ctx:
        def sb(name, shape):
            return ctx.enter_context(nc.sbuf_tensor(name, shape, fp32))

        def sem(name):
            return ctx.enter_context(nc.semaphore(name))

        hT = sb("hT", [P, KC, T])
        xnT = sb("xnT", [P, KC, T])
        W = sb("W", [P, SLOTS, KC, P])
        BIG = sb("BIG", [P, 16384])
        TMP = sb("TMP", [P, 13000])
        cst = sb("cst", [P, C_END])
        prmT = sb("prmT", [P, 6, P])
        modc = sb("modc", [P, 2, 48, 2])
        acol = sb("acol", [P, 2, KC, 2])
        cact = sb("cact", [P, KC, 2])
        small = sb("small", [P, 64])
        dcol = sb("dcol", [P, 2, 16])
        dall = sb("dall", [P, 2, 32])
        rb = sb("rb", [P, T])
        PS = [ctx.enter_context(nc.psum_tensor(f"ps{b}", [P, 512], fp32)) for b in range(8)]

        ident = cst[:, C_ID:C_ID + P]
        upper = cst[:, C_UP:C_UP + P]
        lower = cst[:, C_LO:C_LO + P]
        ones = cst[:, C_ONE:C_ONE + P]

        SBANK = [0, 1, 7]
        DEPTH = len(SBANK)

        def carve(region, *shapes):
            at, views = 0, []
            for shape in shapes:
                n = int(np.prod(shape))
                v = region[:, at:at + n]
                if len(shape) > 1:
                    names = "abcd"[:len(shape)]
                    v = v.rearrange(f"p ({' '.join(names)}) -> p {' '.join(names)}",
                                    **{x: k for x, k in zip(names[1:], shape[1:])})
                views.append(v)
                at += n
            assert at <= region.shape[1], (at, region.shape)
            return views

        xin, rows = carve(BIG, (4, D), (6, P))
        posrow, = carve(TMP, (P,))
        lamv, lamt = carve(TMP[:, 128:], (4, P), (4, HD))
        mix1, biasraw, biasT, = carve(BIG, (KC, S), (16, S), (16, S))
        w1c = BIG[:, 10240:10240 + 32 * P].rearrange("p (l h) -> p l h", h=P)
        hid1, = carve(BIG, (FC1, S))
        (q1, k1, k2, v1, SC, Pb, PT, blk, hidc, kcmp, vcmp, w2c, posT, gate1, gsel, cols, onehot, ffs) = carve(
            TMP, (2, S), (S,), (S,), (2, P), (DEPTH, S), (DEPTH, S), (DEPTH, S), (32, 15), (2, 15), (15,), (HD,),
            (3, HD), (32,), (2, 24), (2, 12), (DEPTH, 4), (LINE,), (2, S))
        lines_c = TMP[0:16, 9000:9000 + LINE]
        lines_b = TMP[0:16, 9400:9400 + LINE]
        yz, attT, mT = carve(BIG, (16, T), (KC, T), (KC, T))
        csb, ecs = carve(BIG[:, 8192:], (2, 4, T), (2, 4, T))
        hid2, = carve(BIG, (FFC, T))
        (tabs, ssq, xpad, xs, xc, xcd, cbm, btm, mt, H, st4, cwc, gd) = carve(
            TMP, (4, 4, 64), (T,), (4, 2, 260), (4, T), (2, 4, S), (2, 4, P), (2, 4, P), (T,), (2, 4, P),
            (2, 3, S), (4, 2, 4, 4), (4, 6), (2, 2))
        y1, zs = carve(TMP[:, 1024 + T:], (2, 520), (2, 520))
        y1, zs = y1[:, :, 0:T], zs[:, :, 0:T]
        dtw = carve(TMP[:, 1600:], (T,), (T,), (T,), (T,), (T,), (T,), (4, HD), (T,))
        (qk, qkt, va, Pa, PTa, cola, osb, osq) = carve(
            TMP[:, 1536:], (2, T), (2, S), (4, P), (DEPTH, T), (DEPTH, T), (DEPTH, 4), (T,), (T,))
        fr, = carve(TMP[:, 1536:], (4, T))
        ogt, = carve(TMP[:, 1536:], (2, D))

        slot_full = [sem(f"slot_full{s}") for s in range(SLOTS)]
        slot_used = [sem(f"slot_used{s}") for s in range(SLOTS)]
        phase_done, load_turn = sem("phase_done"), sem("load_turn")
        in_x, in_c, in_rows, in_w = sem("in_x"), sem("in_c"), sem("in_rows"), sem("in_w")
        in_small = sem("in_small")
        set_t, set_e, set_s = sem("set_transposed"), sem("set_evacuated"), sem("set_small")
        line_ps, line_sb, line_out, bias_in = sem("line_ps"), sem("line_sb"), sem("line_out"), sem("bias_in")
        n_sq, n_sum, n_ms, n_rt, n_x = (sem(f"norm_{x}") for x in ("squares", "sum", "mean", "root", "scaled"))
        u_sc, u_mx, u_ex, u_pn, u_tp, u_pt, u_pv = (
            {k: sem(f"{k}_{x}") for k in ("A", "B", "att0", "att1")}
            for x in ("scores", "max", "exp", "prob", "probT", "probTs", "value"))
        rnd = {k: sem(f"{k}_round") for k in ("A", "B", "ssd0", "ssd1", "att0", "att1", "ada0", "ada1")}
        kept = {k: sem(f"{k}_kept") for k in ("A", "B", "att0", "att1")}
        cmp_s = sem("cmp_steps")
        cmp_e = sem("cmp_evacuated")
        ada_free = sem("modulation_read")
        bl_ready, pool_turn = sem("windows_ready"), sem("pool_turn")
        ssd_ms, ssd_rt = sem("ssd_norm_mean"), sem("ssd_norm_root")
        g_mid, g_free = sem("gemm_activated"), sem("gemm_free")
        rot = {k: sem(f"{k}_rotated") for k in ("att0", "att1")}
        roped = {k: sem(f"{k}_roped") for k in ("att0", "att1")}
        sub_q, sub_p, sub_r = sem("subln_squares"), sem("subln_sum"), sem("subln_root")
        dt_pe, dt_act, dt_dve, cs_out = sem("dt_pe"), sem("dt_act"), sem("dt_dve"), sem("cs_out")
        names = ("padded", "conv", "xs", "gated", "csb", "ecs", "tr", "btm", "xc", "cbm", "states", "h",
                 "cexp", "mmin", "mexp", "mready", "ychunk", "ydone", "y1", "ysq", "ysum")
        ssd = {(l, x): sem(f"ssd{l}_{x}") for l in range(2) for x in names}
        out_t, out_e, out_d = sem("out_transposed"), sem("out_copied"), sem("out_stored")

        tiles_of = {"wout1": 8, "ffn1": 2 * FC1, "down1": 8}
        for l in range(2):
            tiles_of |= {f"merge{l}": 32, f"wout2{l}": 8, f"f1{l}": 32, f"f2{l}": 8}
        g_before, at = {}, 0
        for ph in PHASES:
            if ph in tiles_of:
                g_before[ph] = at
                at += tiles_of[ph]
        ada_before, at = {}, 0
        for ph in ADA:
            ada_before[ph] = at
            at += loads[ph][0]
        units = {"A": softmax_units_a(), "B": softmax_units_b(), "att0": softmax_units_diff(False),
                 "att1": softmax_units_diff(True)}

        def begin(eng, ph):
            if phase_no[ph]:
                eng.wait_ge(phase_done, 3 * phase_no[ph])

        def end(eng):
            eng.drain()
            eng.sem_inc(phase_done, 1)

        def made(eng, ph, s, i):
            eng.wait_ge(slot_used[s], i + (before[ph, s][0] + 2))

        def flat(v):
            return v.rearrange("p a b -> p (a b)")

        def rounds(eng, n):
            return eng.Fori(0, n)

        def wide(l):
            return S if l else T

        def segments(n):
            return [(0, 0, S)] + ([(1, S, T)] if n == T else [])

        block = ctx.enter_context(nc.Block())

        @block.sync
        def _(sp):
            for ph in PHASES:
                if ph not in loads:
                    continue
                times, tiles = loads[ph]

                def bring(i):
                    for s, src in tiles:
                        sp.wait_ge(slot_used[s], i + (before[ph, s][0] + 1))
                        sp.sem_inc(load_turn, 1)
                        for (c0, n, col0, m), ap in src(i):
                            sp.dma_start(W[:, s, c0:c0 + n, col0:col0 + m], ap).then_inc(slot_full[s], 16)

                if times > 1:
                    with rounds(sp, times) as i:
                        bring(i)
                else:
                    bring(0)
            for t in range(2):
                sp.wait_ge(out_e, t + 1)
                sp.dma_start(out[0, t * P:(t + 1) * P, :], ogt[:, t, :]).then_inc(out_d, 16)
            sp.wait_ge(out_d, 32)

        @block.gpsimd
        def _(pool):
            pool.dma_start(cst[:, :], a["const"]).then_inc(in_c, 16)
            for n, name in enumerate(("x", "ctx_2")):
                pool.dma_start(xin[:, 2 * n:2 * n + 2, :], a[name][0].rearrange("(t p) d -> p t d", p=P)).then_inc(in_x, 16)

            def row(name, src):
                g, r = PARAM_ROWS[name]
                n = src.shape[0]
                pool.dma_start(rows[r:r + n, g, :], src).then_inc(in_rows, 16)

            def vec(v):
                return v.rearrange("(r p) -> r p", p=P)

            for name in ("norm1_g", "norm2_g"):
                row(name, vec(a[name][0]))
            row("norm_f_g", vec(a["norm_f_g"]))
            row("final", vec(a["final_norm_g_2"]))
            row("c", vec(a["c_2"][0]))
            row("cctx", vec(a["c_ctx_2"]))
            row("kb1", vec(a["cmp_k_b1"][0]))
            row("vb1", vec(a["cmp_v_b1"][0]))
            for l in range(2):
                row(f"mix{l}", vec(a["norm_mix_g_2"][l]))
                row(f"mlp{l}", vec(a["norm_mlp_g_2"][l]))
                row(f"ssdg{l}", vec(a["ssd_norm_g_2"][l]))
                row(f"subln{l}", vec(a["attn_subln_g_2"][l]))
                row(f"ada{l}", vec(a["ada_b_2"][l]))
                row(f"cwA{l}", a["conv_w_2"][l, 0:3].rearrange("k (r p) -> (k r) p", p=P))
                row(f"cwB{l}", a["conv_w_2"][l, 3:5].rearrange("k (r p) -> (k r) p", p=P))
                row(f"cb{l}", vec(a["conv_b_2"][l]))
            for d in range(2):
                pool.dma_start(posrow[0:32, 64 * d:64 * d + 64], a["cmp_pos"][0]).then_inc(in_rows, 16)
            for l in range(2):
                for d, x in enumerate("fb"):
                    pool.dma_start(small[32 * d:32 * d + 32, l:l + 1],
                                   a[f"dt_bias_{x}_2"][l].rearrange("(h o) -> h o", o=1)).then_inc(in_small, 16)
                    pool.dma_start(small[32 * d:32 * d + 32, 2 + l:3 + l],
                                   a[f"a_log_{x}_2"][l].rearrange("(h o) -> h o", o=1)).then_inc(in_small, 16)
            pool.dma_start(flat(dall), a["ssd_d_2"].rearrange("(o l) h -> o (l h)", o=1).to_broadcast([P, 64]))\
                .then_inc(in_small, 16)
            for k, x in enumerate(("q1", "k1", "q2", "k2")):
                pool.dma_start(lamv[:, k, :], a[f"lambda_{x}_2"].rearrange("(o l) d -> o (l d)", o=1)
                               .to_broadcast([P, P])).then_inc(in_small, 16)
            begin(pool, "bias")
            pool.dma_start(onehot[0:32, :], a["onehot"]).then_inc(in_w, 16)
            pool.dma_start(lines_c, a["lines"]).then_inc(in_w, 16)
            pool.dma_start(small[0:32, 32:48], a["rel_bias"]).then_inc(in_w, 16)
            for d, x in enumerate("kv"):
                pool.dma_start(w1c[64 * d:64 * d + 64, :, :], a[f"cmp_{x}_w1"][0].rearrange("l d h -> d l h"))\
                    .then_inc(in_w, 16)
            for n, x in enumerate("kkv"):
                pool.dma_start(w2c[:, n, :], a[f"cmp_{x}_w2"][0]).then_inc(in_w, 16)
            pool.wait_ge(line_sb, 1)
            pool.dma_start(line_dram[:, :], lines_b).then_inc(line_out, 16)
            pool.wait_ge(line_out, 16)
            pool.dma_start(biasraw, bass.AP(tensor=line_dram, offset=0, ap=[[1, P], [LINE, 16], [1, S]]))\
                .then_inc(bias_in, 16)
            for l in range(2):
                pool.wait_ge(dt_dve, 9 * l + 9)
                pool.dma_start(cs_dram[:, :], dtw[7][0:64, :]).then_inc(cs_out, 16)
                pool.wait_ge(cs_out, 16 * (l + 1))
                begin(pool, f"ssd{l}")
                with rounds(pool, NG) as g:
                    pool.wait_ge(rnd[f"ssd{l}"], g * 3 + 3)
                    pool.sem_inc(pool_turn, 1)
                    for d in range(2):
                        pool.dma_start(
                            csb[:, d, :, :],
                            cs_dram[bass.ds(g * 4 + 32 * d, 4), :].rearrange("h t -> (h t)")
                            .rearrange("(o h t) -> o h t", o=1, h=4).to_broadcast([P, 4, T])).then_inc(ssd[l, "csb"], 16)

        @block.scalar
        def _(act):
            A = nc.scalar.activation

            def copy(dst, src):
                return A(dst, src, ACT.Copy)

            def squares(name, n):
                k = NORMS.index(name)
                begin(act, name)
                for c in range(KC):
                    A(xnT[:, c, 0:n], hT[:, c, 0:n], ACT.Square).then_inc(n_sq, 1)
                act.wait_ge(n_ms, k + 1)
                A(rb[:, 0:n], rb[:, 0:n], ACT.Sqrt).then_inc(n_rt, 1)

            def shifted(name, l, which, n):
                squares(name, n)
                k = NORMS.index(name)
                for c in range(KC):
                    act.wait_ge(n_x, 8 * k + c + 1)
                    for m, lo, hi in segments(n):
                        A(xnT[:, c, lo:hi], xnT[:, c, lo:hi], ACT.Identity, bias=modc[:, l, 24 * which + c, m:m + 1])
                end(act)

            def soft(name, i, n_units, u, w, pbuf, ptbuf, src, scale, colt):
                base = i * n_units
                act.wait_ge(u_mx[name], base + (w + 1))
                A(pbuf[:, w % DEPTH, 0:u["nk"]], src, ACT.Exp, bias=colt[:, w % DEPTH, 0:1], scale=scale,
                  accum_out=colt[:, w % DEPTH, 1:2]).then_inc(u_ex[name], 1)

            def soft_t(name, i, n_units, u, w, ptbuf):
                act.wait_ge(u_tp[name], i * n_units + (w + 1))
                nk = u["nk"]
                if nk < P:
                    copy(ptbuf[0:nk, w % DEPTH, 0:P], PS[2][0:nk, 0:P]).then_inc(u_pt[name], 1)
                else:
                    copy(ptbuf[:, w % DEPTH, 0:nk], PS[2][:, 0:nk]).then_inc(u_pt[name], 1)

            def soft_all(name, i, src_of, scale, pbuf, ptbuf, colt):
                us = units[name]
                ahead = DEPTH - 1
                for w in range(len(us) + ahead):
                    if w < len(us):
                        soft(name, i, len(us), us[w], w, pbuf, ptbuf, src_of(us[w], w), scale, colt)
                    if w >= ahead:
                        soft_t(name, i, len(us), us[w - ahead], w - ahead, ptbuf)

            for n in range(8):
                act.wait_ge(set_t, n + 1)
                copy(hT[:, n, :], PS[n % 4][:, :]).then_inc(set_e, 1)
            for g in range(6):
                act.wait_ge(set_t, 9 + g)
                copy(prmT[:, g, 0:PARAM_SIZE[g]], PS[4 + g % 4][:, 0:PARAM_SIZE[g]]).then_inc(set_e, 1)
            act.wait_ge(set_t, 15)
            copy(posT[:, :], PS[3][:, 0:32]).then_inc(set_e, 1)
            act.drain()
            A(cact[:, :, :], prmT[:, 0, 96:112].rearrange("p (m c) -> p c m", m=2), ACT.Silu)
            act.wait_ge(in_small, 16 * 13)
            A(small[0:64, 2:4], small[0:64, 2:4], ACT.Exp)
            act.wait_ge(set_s, 1)
            A(small[:, 12:16], small[:, 8:12], ACT.Exp).then_inc(set_s, 1)
            end(act)

            begin(act, "bias")
            end(act)
            squares("norm1", S)
            end(act)

            begin(act, "A")
            with rounds(act, 4) as i:
                act.wait_ge(rnd["A"], i * 3 + 3)
                for n, dst in enumerate((q1[:, 0, :], k1, flat(v1))):
                    made(act, "A", n, i)
                    copy(dst, PS[4 + n][:, 0:S]).then_inc(kept["A"], 1)
                soft_all("A", i, lambda u, w: SC[:, w % DEPTH, 0:u["nk"]], 1.0, Pb, PT, cols)
                act.drain()
                act.sem_inc(rnd["A"], 1)
            end(act)

            begin(act, "B")
            with rounds(act, 2) as g:
                act.wait_ge(rnd["B"], g * 3 + 3)
                made(act, "B", 3, g)
                A(flat(gate1), PS[4][:, 0:48], ACT.Sigmoid).then_inc(kept["B"], 1)
                for n, (dst, b, k) in enumerate((
                        (q1[:, 0, :], 5, S), (q1[:, 1, :], 6, S), (k1, 4, S), (k2, 5, S), (flat(v1), 6, S))):
                    made(act, "B", [4, 5, 7, 8, 9][n], g)
                    copy(dst, PS[b][:, 0:k]).then_inc(kept["B"], 1)
                for n, prm in enumerate(("kb1", "vb1")):
                    col = PARAM_ROWS[prm][1]
                    act.wait_ge(cmp_s, g * 4 + (n + 1))
                    A(hidc[:, n, :], PS[3 * n][:, 0:15], ACT.Gelu_apprx_tanh,
                      bias=prmT[:, 0, col:col + 1]).then_inc(cmp_e, 1)
                act.wait_ge(cmp_s, g * 4 + 4)
                copy(kcmp[:, :], PS[1][:, 0:15]).then_inc(cmp_e, 1)
                copy(vcmp[0:15, :], PS[2][0:15, 0:64]).then_inc(cmp_e, 1)
                soft_all("B", g, lambda u, w: SC[:, w % DEPTH, 0:u["nk"]], 1.0, Pb, PT, cols)
                act.drain()
                act.sem_inc(rnd["B"], 1)
            end(act)

            begin(act, "wout1")
            end(act)
            squares("norm2", S)
            end(act)
            begin(act, "ffn1")
            with rounds(act, FC1 // 2) as i:
                for n in range(2):
                    made(act, "ffn1", 4 + 2 * n, i)
                    act.wait_ge(g_free, i * 4 + (g_before["ffn1"] + 2 * n + 2))
                    A(ffs[:, n, :], PS[4 + 2 * n][:, 0:S], ACT.Silu).then_inc(g_mid, 1)
            end(act)
            begin(act, "down1")
            end(act)
            squares("normf1", S)
            end(act)

            for l in range(2):
                n_tok = wide(l)
                begin(act, f"ada{l}")
                end(act)
                shifted(f"mixnorm{l}", l, 0, T)

                begin(act, f"dt{l}")
                xb, ax, e, den, z, w2, tot, csr = dtw
                act.wait_ge(dt_dve, 9 * l + 1)
                A(e[0:64, :], ax[0:64, :], ACT.Exp, scale=-1.0).then_inc(dt_act, 1)
                act.wait_ge(dt_pe, 6 * l + 2)
                copy(flat(tabs[:, 0, :, :]), PS[5][:, 0:256]).then_inc(dt_act, 1)
                act.wait_ge(dt_pe, 6 * l + 3)
                copy(flat(tot), PS[6][:, 0:256]).then_inc(dt_act, 1)
                act.wait_ge(dt_pe, 6 * l + 6)
                A(flat(tabs[:, 3, :, :]), PS[3][:, 0:256], ACT.Exp).then_inc(dt_act, 1)
                act.wait_ge(dt_dve, 9 * l + 8)
                act.drain()
                A(tabs[:, 1, :, :], tabs[:, 1, :, :], ACT.Exp).then_inc(dt_act, 1)
                end(act)

                begin(act, f"ssd{l}")
                with rounds(act, NG) as g:
                    R = lambda x, k, n: act.wait_ge(ssd[l, x], g * k + n)
                    act.wait_ge(rnd[f"ssd{l}"], g * 3 + 3)
                    for t in range(4):
                        made(act, f"ssd{l}", [9, 0, 1, 2][t], g)
                        copy(xpad[:, t, :, 2:258], PS[[6, 7, 0, 1][t]][:, :].rearrange("p (s n) -> p s n", s=2))\
                            .then_inc(ssd[l, "padded"], 1)
                    for t in range(4):
                        R("conv", 4, t + 1)
                        A(xs[:, t, :], xs[:, t, :], ACT.Silu, bias=cwc[:, t, 5:6]).then_inc(ssd[l, "xs"], 1)
                    for t in range(2):
                        made(act, f"ssd{l}", 3 + t, g)
                        A(zs[:, t, 0:n_tok], PS[2 + t][:, 0:n_tok], ACT.Silu).then_inc(ssd[l, "gated"], 1)
                    R("tr", 2, 1)
                    copy(btm[:, :], PS[6][:, :]).then_inc(ssd[l, "btm"], 1)
                    R("csb", 32, 32)
                    A(ecs[:, :, :, :], csb[:, :, :, :], ACT.Exp).then_inc(ssd[l, "ecs"], 1)
                    n_ch = n_tok // P
                    for ch in range(n_ch):
                        for d in range(2):
                            R("mmin", 2 * n_ch, 2 * ch + d + 1)
                            A(mt[:, d, :, :], mt[:, d, :, :], ACT.Exp).then_inc(ssd[l, "mexp"], 1)
                    for t in range(2):
                        R("y1", 2, t + 1)
                        A(zs[:, t, 0:n_tok], y1[:, t, 0:n_tok], ACT.Square).then_inc(ssd[l, "ysq"], 1)
                    act.drain()
                    act.sem_inc(rnd[f"ssd{l}"], 1)
                act.wait_ge(ssd_ms, l + 1)
                A(ssq[:, 0:n_tok], ssq[:, 0:n_tok], ACT.Sqrt).then_inc(ssd_rt, 1)
                end(act)

                name = f"att{l}"
                begin(act, name)
                with rounds(act, 8) as h:
                    act.wait_ge(rnd[name], h * 3 + 3)
                    for n, (dst, k) in enumerate(((qk[:, 0, 0:n_tok], n_tok), (qk[:, 1, :], T), (flat(va), T))):
                        made(act, name, 5 + n, h)
                        copy(dst, PS[4 + n][:, 0:k]).then_inc(kept[name], 1)
                    soft_all(name, h, lambda u, w: PS[SBANK[w % DEPTH]][:, 0:u["nk"]], HD ** -0.5, Pa, PTa, cola)
                    act.drain()
                    act.sem_inc(rnd[name], 1)
                for h in range(8):
                    if h >= 1:
                        act.wait_ge(sub_p, 8 * l + h)
                    else:
                        act.wait_ge(rnd[name], 27)
                    A(osq[:, 0:n_tok], attT[:, h, 0:n_tok], ACT.Square).then_inc(sub_q, 1)
                    act.wait_ge(sub_r, 16 * l + 2 * h + 1)
                    A(osb[:, 0:n_tok], osb[:, 0:n_tok], ACT.Sqrt).then_inc(sub_r, 1)
                end(act)

                begin(act, f"merge{l}")
                with rounds(act, 8) as i:
                    b = g_before[f"merge{l}"]
                    for n in range(2):
                        made(act, f"merge{l}", 8 + n, i)
                        act.wait_ge(g_free, i * 4 + (b + 4))
                        A(fr[:, n, 0:n_tok], PS[4 + n][:, 0:n_tok], ACT.Sigmoid).then_inc(g_mid, 1)
                end(act)
                begin(act, f"wout2{l}")
                end(act)
                shifted(f"mlpnorm{l}", l, 1, n_tok)
                begin(act, f"f1{l}")
                with rounds(act, 8) as i:
                    b = g_before[f"f1{l}"]
                    for n in range(4):
                        made(act, f"f1{l}", [7, 8, 9, 0][n], i)
                        act.wait_ge(g_free, i * 4 + (b + n + 1))
                        A(fr[:, n, 0:n_tok], PS[4 + n][:, 0:n_tok], ACT.Relu).then_inc(g_mid, 1)
                end(act)
                begin(act, f"f2{l}")
                end(act)
            squares("normend", S)
            end(act)
            begin(act, "out")
            for t in range(2):
                for half in range(2):
                    act.wait_ge(out_t, 2 * t + half + 1)
                    k = copy(ogt[:, t, 512 * half:512 * half + 512], PS[2 * t + half][:, :])
                k.then_inc(out_e, 1)
            end(act)

        @block.tensor
        def _(pe):
            mm = nc.tensor.matmul

            def product(ph, i, slots, dst, rhs, m=P, col0=0):
                times, tiles = loads[ph]
                sizes = {s: src(0)[0][0][1] for s, src in tiles}
                total = sum(sizes[s] for s in slots)
                k = 0
                for s in slots:
                    pe.wait_ge(slot_full[s], i * per_fill[ph, s] + (before[ph, s][1] + per_fill[ph, s]))
                    for c in range(sizes[s]):
                        last = mm(dst, W[:, s, c, col0:col0 + m], rhs(k), start=k == 0, stop=k == total - 1)
                        k += 1
                    last.then_inc(slot_used[s], 1)
                return last

            def token_major(ph, i, s, dst, tiles, width, col0=0, give=True):
                pe.wait_ge(slot_full[s], i * per_fill[ph, s] + (before[ph, s][1] + per_fill[ph, s]))
                for t in range(tiles):
                    for c in range(KC):
                        last = mm(dst(t), xnT[:, c, t * P:(t + 1) * P], W[:, s, c, col0:col0 + width],
                                  start=c == 0, stop=c == KC - 1)
                if give:
                    last.then_inc(slot_used[s], 1)
                return last

            def ada(ph, i):
                if ph in ADA:
                    l, slots, _, bank = ADA[ph]
                    pe.wait_ge(ada_free, i + (ada_before[ph] + 1))
                    for t, s in enumerate(slots):
                        product(ph, i, [s], PS[bank][:, 2 * t:2 * t + 2], lambda k: cact[:, k, :])

            def norm(name, n):
                k = NORMS.index(name)
                begin(pe, name)
                for c in range(KC):
                    pe.wait_ge(n_sq, 8 * k + c + 1)
                    last = mm(PS[0][:, 0:n], ones, xnT[:, c, 0:n], start=c == 0, stop=c == KC - 1)
                last.then_inc(n_sum, 1)
                end(pe)

            def scores(name, i, u, w, qa, ka):
                n = len(units[name])
                if w >= DEPTH:
                    pe.wait_ge(u_ex[name], i * n + (w - DEPTH + 1))
                lo = u["part"]
                mm(PS[SBANK[w % DEPTH]][:, 0:u["nk"]], qa, ka, start=True, stop=True).then_inc(u_sc[name], 1)

            def values(name, i, u, w, pbuf, ptbuf, v, obank):
                n = len(units[name])
                nk = u["nk"]
                pe.wait_ge(u_pn[name], i * n + (w + 1))
                kbs = max(nk // P, 1)
                for kb in range(kbs):
                    r = min(nk, P)
                    last = nc.tensor.transpose(PS[2][0:r, kb * P:(kb + 1) * P], pbuf[:, w % DEPTH, kb * P:kb * P + r], ident)
                last.then_inc(u_tp[name], 1)
                pe.wait_ge(u_pt[name], i * n + (w + 1))
                part, col = u["out"]
                for kb in range(kbs):
                    r = min(nk, P)
                    last = mm(PS[obank][part:part + v(kb).shape[1], col:col + P], v(kb), ptbuf[0:r, w % DEPTH, kb * P:(kb + 1) * P],
                              start=u["first"] and kb == 0, stop=u["last"] and kb == kbs - 1)
                last.then_inc(u_pv[name], 1)

            def soft_all(name, i, qk_of, v_of, pbuf, ptbuf, obank, between={}):
                us = units[name]
                ahead = DEPTH - 1
                for w in range(ahead):
                    scores(name, i, us[w], w, *qk_of(us[w]))
                for w, u in enumerate(us):
                    if w + ahead < len(us):
                        scores(name, i, us[w + ahead], w + ahead, *qk_of(us[w + ahead]))
                    if w in between:
                        between[w]()
                    values(name, i, u, w, pbuf, ptbuf, v_of(u), obank)

            for s in range(SLOTS):
                pe.sem_inc(slot_used[s], 1)
            pe.wait_ge(in_c, 16)
            pe.wait_ge(in_x, 32)
            for n in range(8):
                if n >= 4:
                    pe.wait_ge(set_e, n - 3)
                for t in range(4):
                    last = nc.tensor.transpose(PS[n % 4][:, t * P:(t + 1) * P], xin[:, t, n * P:(n + 1) * P], ident)
                last.then_inc(set_t, 1)
            pe.wait_ge(in_rows, 16 * 26)
            for g in range(6):
                k = PARAM_SIZE[g]
                if g >= 4:
                    pe.wait_ge(set_e, 8 + g - 3)
                nc.tensor.transpose(PS[4 + g % 4][:, 0:k], rows[0:k, g, :], ident[0:k, 0:k]).then_inc(set_t, 1)
            pe.wait_ge(set_e, 8)
            nc.tensor.transpose(PS[3][:, 0:32], posrow[0:32, :], ident[0:32, 0:32]).then_inc(set_t, 1)
            end(pe)

            begin(pe, "bias")
            pe.wait_ge(in_w, 16 * 8)
            mm(PS[0][0:16, 0:LINE], small[0:32, 32:48], onehot[0:32, :], start=True, stop=True).then_inc(line_ps, 1)
            end(pe)

            norm("norm1", S)

            x1 = lambda k: xnT[:, k, 0:S]
            begin(pe, "A")

            def a_front(i):
                return [lambda: product("A", i, [0], PS[4][:, 0:S], x1), lambda: product("A", i, [1], PS[5][:, 0:S], x1),
                        lambda: token_major("A", i, 2, lambda t: PS[6][:, t * P:(t + 1) * P], 2, P)]

            def a_back(i, more):
                pe.wait_ge(rnd["A"], i * 3 + 3)
                ada("A", i)
                pe.wait_ge(kept["A"], i * 3 + 3)
                soft_all("A", i, lambda u: (q1[u["part"]:u["part"] + 64, 0, u["q"]:u["q"] + P],
                                            k1[u["part"]:u["part"] + 64, 0:u["nk"]]),
                         lambda u: (lambda kb: v1[:, kb, u["part"]:u["part"] + 64]), Pb, PT, 3,
                         dict(zip((0, 1, 2), a_front(i + 1))) if more else {})
                pe.drain()
                pe.sem_inc(rnd["A"], 1)

            for f in a_front(0):
                f()
            with rounds(pe, 3) as i:
                a_back(i, True)
            a_back(3, False)
            end(pe)

            begin(pe, "B")
            with rounds(pe, 2) as g:
                pe.wait_ge(rnd["B"], g * 3 + 3)
                token_major("B", g, 3, lambda t: PS[4][:, t * 24:t * 24 + 24], 2, 24)
                product("B", g, [4], PS[5][:, 0:S], x1)
                product("B", g, [5], PS[6][:, 0:S], x1)
                product("B", g, [6], PS[7][:, 0:S], x1)
                pe.wait_ge(kept["B"], g * 6 + 1)
                product("B", g, [7], PS[4][:, 0:S], x1)
                pe.wait_ge(kept["B"], g * 6 + 2)
                product("B", g, [8], PS[5][:, 0:S], x1)
                pe.wait_ge(kept["B"], g * 6 + 3)
                token_major("B", g, 9, lambda t: PS[6][:, t * P:(t + 1) * P], 2, P)
                pe.wait_ge(kept["B"], g * 6 + 6)
                pe.wait_ge(bl_ready, g + 1)
                for n in range(2):
                    for j in range(32):
                        last = mm(PS[3 * n][:, 0:15], w1c[64 * n:64 * n + 64, j, :], blk[64 * n:64 * n + 64, j, :],
                                  start=j == 0, stop=j == 31)
                    last.then_inc(cmp_s, 1)
                pe.wait_ge(cmp_e, g * 4 + 2)
                mm(PS[1][:, 0:15], flat(w2c[:, 0:2, :]), hidc[:, 0, :], start=True, stop=True).then_inc(cmp_s, 1)
                mm(PS[2][0:15, 0:64], hidc[:, 1, :], w2c[:, 2, :], start=True, stop=True).then_inc(cmp_s, 1)
                pe.wait_ge(cmp_e, g * 4 + 4)

                def operands(u):
                    q = q1[u["part"]:u["part"] + 64, u["head"] // 2, u["q"]:u["q"] + P]
                    return q, [kcmp, k1, k2][u["branch"]][u["part"]:u["part"] + 64, 0:u["nk"]]

                def vals(u):
                    br = u["branch"]
                    return (lambda kb: vcmp[0:15, :]) if br == 0 else (
                        lambda kb: v1[:, kb, 64 * (br - 1):64 * br])

                soft_all("B", g, operands, vals, Pb, PT, 3)
                pe.drain()
                pe.sem_inc(rnd["B"], 1)
            end(pe)

            def tiles(ph, times, slot_sets, dst, rhs):
                begin(pe, ph)
                b = g_before[ph]
                n = len(slot_sets)
                with rounds(pe, times) as i:
                    for t, slots in enumerate(slot_sets):
                        pe.wait_ge(g_free, i * n + (b + t + 5 - n))
                        product(ph, i, slots, dst(t), rhs(t))
                    ada(ph, i)
                end(pe)

            tiles("wout1", 2, [[0], [1], [2], [3]], lambda t: PS[4 + t][:, 0:S], lambda t: lambda k: mix1[:, k, :])
            norm("norm2", S)
            tiles("ffn1", FC1 // 2, [[4], [5], [6], [7]], lambda t: PS[4 + t][:, 0:S], lambda t: x1)
            tiles("down1", 4, [[8, 9, 0], [1, 2, 3]], lambda t: PS[4 + t][:, 0:S], lambda t: lambda k: hid1[:, k, :])
            norm("normf1", S)

            for l in range(2):
                nt = wide(l)
                xa = lambda k: xnT[:, k, :]
                xn = lambda k: xnT[:, k, 0:nt]
                begin(pe, f"ada{l}")
                end(pe)
                norm(f"mixnorm{l}", T)

                begin(pe, f"dt{l}")
                product(f"dt{l}", 0, [8], PS[4][0:64, :], xa, 64)
                pe.drain()
                pe.sem_inc(dt_pe, 1)
                xb, ax, e, den, z, w2, tot, csr = dtw
                pe.wait_ge(dt_dve, 9 * l + 3)
                for ch in range(4):
                    last = nc.tensor.transpose(PS[5][:, 64 * ch:64 * ch + 64], xb[0:64, ch * P:(ch + 1) * P], ident[0:64, 0:64])
                last.then_inc(dt_pe, 1)
                for ch in range(4):
                    last = nc.tensor.transpose(PS[6][:, 64 * ch:64 * ch + 64], ax[0:64, ch * P:(ch + 1) * P], ident[0:64, 0:64])
                last.then_inc(dt_pe, 1)
                pe.wait_ge(dt_act, 5 * l + 3)
                for ch in range(4):
                    for d, tri in enumerate((upper, lower)):
                        last = mm(PS[7][32 * d:32 * d + 32, ch * P:(ch + 1) * P], tot[:, ch, 32 * d:32 * d + 32], tri,
                                  start=True, stop=True)
                last.then_inc(dt_pe, 1)
                for ch in range(4):
                    for d, tri in enumerate((upper, lower)):
                        last = mm(PS[0][:, 64 * ch + 32 * d:64 * ch + 32 * d + 32], tri, tot[:, ch, 32 * d:32 * d + 32],
                                  start=True, stop=True)
                last.then_inc(dt_pe, 1)
                mm(PS[3][:, 0:256], ones, flat(tot), start=True, stop=True).then_inc(dt_pe, 1)
                end(pe)

                begin(pe, f"ssd{l}")
                ph = f"ssd{l}"

                def front(g, t):
                    product(ph, g, [(9, 0, 1, 2)[t]], PS[[6, 7, 0, 1][t]][:, :], xa)

                def back(g, more):
                    R = lambda x, k, n: pe.wait_ge(ssd[l, x], g * k + n)
                    pe.wait_ge(rnd[ph], g * 3 + 3)
                    for t, s in enumerate((3, 4)):
                        product(ph, g, [s], PS[2 + t][:, 0:nt], xn)
                    ada(ph, g)
                    R("xs", 4, 4)
                    for ch in range(4):
                        nc.tensor.transpose(PS[6][:, ch * P:(ch + 1) * P], xs[:, 2, ch * P:(ch + 1) * P], ident)
                        for t in range(2):
                            last = nc.tensor.transpose(PS[4 + ch // 2][:, (ch % 2) * S + t * P:(ch % 2) * S + (t + 1) * P],
                                                       xs[:, t, ch * P:(ch + 1) * P], ident)
                    last.then_inc(ssd[l, "tr"], 1)
                    for ch in range(4):
                        last = mm(PS[7][:, ch * P:(ch + 1) * P], xs[:, 2, ch * P:(ch + 1) * P],
                                  xs[:, 3, ch * P:(ch + 1) * P], start=True, stop=True)
                    last.then_inc(ssd[l, "tr"], 1)
                    if more:
                        front(g + 1, 2)
                    R("btm", 1, 1)
                    R("gated", 2, 2)
                    for step in range(3):
                        R("xc", 6, 2 * step + 2)
                        if step == 2:
                            R("h", 3, 1)
                        for d, order in enumerate((FWD, BWD)):
                            ch = order[step]
                            last = mm(PS[[2, 3, 2][step]][:, d * S:(d + 1) * S], btm[:, ch * P:(ch + 1) * P],
                                      xcd[:, d, :, :].rearrange("p h c -> p (h c)")[:, (step % 2) * S:(step % 2) * S + S],
                                      start=True, stop=True)
                        last.then_inc(ssd[l, "states"], 1)
                        if more and step == 1:
                            front(g + 1, 3)
                    if more:
                        front(g + 1, 0)
                    R("h", 3, 3)
                    R("cexp", 2, 2)
                    n_ch = nt // P
                    for ch in range(n_ch):
                        R("mready", 2 * n_ch, 2 * ch + 2)
                        for h in range(4):
                            dst = PS[4 + h // 2][64 * (h % 2):64 * (h % 2) + 64, ch * P:(ch + 1) * P]
                            parts = [(xc[:, d, ch, h * HD:(h + 1) * HD], mt[:, d, h, :]) for d in range(2)]
                            for d, order in enumerate((FWD, BWD)):
                                k = order.index(ch)
                                if k:
                                    parts.append((H[:, d, k - 1, h * HD:(h + 1) * HD], ecs[:, d, h, ch * P:(ch + 1) * P]))
                            for n, (lhs, rhs) in enumerate(parts):
                                last = mm(dst, lhs, rhs, start=n == 0, stop=n == len(parts) - 1)
                        last.then_inc(ssd[l, "ychunk"], 1)
                    if more:
                        R("cbm", 1, 1)
                        front(g + 1, 1)
                    for t in range(2):
                        R("ysq", 2, t + 1)
                        last = mm(PS[2][:, 0:nt], ones, zs[:, t, 0:nt], start=t == 0, stop=t == 1)
                    last.then_inc(ssd[l, "ysum"], 1)
                    pe.drain()
                    pe.sem_inc(rnd[ph], 1)

                for t in range(4):
                    front(0, t)
                with rounds(pe, NG - 1) as g:
                    back(g, True)
                back(NG - 1, False)
                end(pe)

                ph = f"att{l}"
                begin(pe, ph)

                def front(h):
                    return [lambda: product(ph, h, [5], PS[4][:, 0:nt], xn), lambda: product(ph, h, [6], PS[5][:, :], xa),
                            lambda: token_major(ph, h, 7, lambda t: PS[6][:, t * P:(t + 1) * P], 4, P)]

                def back(h, more):
                    pe.wait_ge(rnd[ph], h * 3 + 3)
                    ada(ph, h)
                    pe.wait_ge(kept[ph], h * 3 + 2)
                    for n in range(2):
                        last = mm(PS[7][:, n * S:(n + 1) * S], cst[:, C_PERM:C_PERM + P], qk[:, n, 0:S], start=True, stop=True)
                    last.then_inc(rot[ph], 1)
                    pe.wait_ge(kept[ph], h * 3 + 3)
                    if more:
                        front(h + 1)[2]()
                    pe.wait_ge(roped[ph], h + 1)
                    soft_all(ph, h, lambda u: (qk[u["part"]:u["part"] + 64, 0, u["q"]:u["q"] + P],
                                               qk[u["part"]:u["part"] + 64, 1, u["k0"]:u["k0"] + u["nk"]]),
                             lambda u: (lambda kb: va[:, u["k0"] // P + kb, :]), Pa, PTa, 3,
                             dict(zip((0, 2) if l else (1, 4), front(h + 1)[:2])) if more else {})
                    pe.drain()
                    pe.sem_inc(rnd[ph], 1)

                for f in front(0):
                    f()
                with rounds(pe, 7) as h:
                    back(h, True)
                back(7, False)
                for h in range(8):
                    pe.wait_ge(sub_q, 8 * l + h + 1)
                    mm(PS[0][:, 0:nt], ones, osq[:, 0:nt], start=True, stop=True).then_inc(sub_p, 1)
                    pe.wait_ge(sub_r, 16 * l + 2 * h + 1)
                end(pe)

                rhs_of = [xn, xn, lambda k: attT[:, k, 0:nt], lambda k: yz[:, k, 0:nt]]
                tiles(f"merge{l}", 8, [[8], [9], [0], [1, 2]], lambda t: PS[4 + t][:, 0:nt], lambda t: rhs_of[t])
                tiles(f"wout2{l}", 2, [[3], [4], [5], [6]], lambda t: PS[4 + t][:, 0:nt], lambda t: lambda k: mT[:, k, 0:nt])
                norm(f"mlpnorm{l}", nt)
                tiles(f"f1{l}", 8, [[7], [8], [9], [0]], lambda t: PS[4 + t][:, 0:nt], lambda t: xn)
                tiles(f"f2{l}", 4, [[1, 2, 3, 4], [5, 6, 7, 8]], lambda t: PS[4 + t][:, 0:nt],
                      lambda t: lambda k: hid2[:, k, 0:nt])
            norm("normend", S)
            begin(pe, "out")
            for t in range(2):
                for half in range(2):
                    for c in range(4):
                        last = nc.tensor.transpose(PS[2 * t + half][:, c * P:(c + 1) * P],
                                                   xnT[:, 4 * half + c, t * P:(t + 1) * P], ident)
                    last.then_inc(out_t, 1)
            end(pe)

        @block.vector
        def _(dve):
            V = nc.vector

            def prm(name, n=1, k=0):
                g, r = PARAM_ROWS[name]
                return prmT[:, g, r + k:r + k + n]

            def norm(name, n, gain):
                k = NORMS.index(name)
                begin(dve, name)
                dve.wait_ge(n_sum, k + 1)
                V.tensor_scalar(rb[:, 0:n], PS[0][:, 0:n], 1.0 / D, EPS, ALU.mult, ALU.add).then_inc(n_ms, 1)
                dve.wait_ge(n_rt, k + 1)
                V.reciprocal(rb[:, 0:n], rb[:, 0:n])
                dve.drain()
                for c in range(KC):
                    for m, lo, hi in segments(n):
                        last = V.scalar_tensor_tensor(out=xnT[:, c, lo:hi], in0=hT[:, c, lo:hi], scalar=gain(c, m),
                                                      in1=rb[:, lo:hi], op0=ALU.mult, op1=ALU.mult)
                    last.then_inc(n_x, 1)
                end(dve)

            def ada(ph, i):
                if ph in ADA:
                    l, slots, first, bank = ADA[ph]
                    n = len(slots)
                    made(dve, ph, slots[-1], i)
                    V.tensor_tensor(modc[:, l, bass.ds(i * n + first, n), :],
                                    PS[bank][:, 0:2 * n].rearrange("p (t m) -> p t m", m=2),
                                    prmT[:, 1, bass.ds(i * n + (first + 48 * l), n)].unsqueeze(2).to_broadcast([P, n, 2]),
                                    ALU.add).then_inc(ada_free, 1)

            def soft_all(name, i, pbuf, colt, bias_of, scale_of):
                us = units[name]
                n = len(us)

                def maximum(u, w):
                    nk = u["nk"]
                    dve.drain()
                    dve.wait_ge(u_sc[name], i * n + (w + 1))
                    if bias_of is None:
                        V.reduce_max(colt[:, w % DEPTH, 2:3], PS[SBANK[w % DEPTH]][:, 0:nk], AX.X)
                        factor = -HD ** -0.5
                    else:
                        V.scalar_tensor_tensor(out=SC[:, w % DEPTH, 0:nk], in0=PS[SBANK[w % DEPTH]][:, 0:nk], scalar=HD ** -0.5,
                                               in1=bias_of(u), op0=ALU.mult, op1=ALU.add)
                        dve.drain()
                        V.reduce_max(colt[:, w % DEPTH, 2:3], SC[:, w % DEPTH, 0:nk], AX.X)
                        factor = -1.0
                    dve.drain()
                    V.tensor_scalar(colt[:, w % DEPTH, 0:1], colt[:, w % DEPTH, 2:3], -1e20, factor, ALU.max, ALU.mult)\
                        .then_inc(u_mx[name], 1)

                ahead = DEPTH - 1
                for w in range(ahead):
                    maximum(us[w], w)
                for w, u in enumerate(us):
                    if w + ahead < n:
                        maximum(us[w + ahead], w + ahead)
                    dve.wait_ge(u_ex[name], i * n + (w + 1))
                    V.tensor_scalar(colt[:, w % DEPTH, 3:4], colt[:, w % DEPTH, 1:2], 1e-30, None, ALU.max)
                    dve.drain()
                    V.reciprocal(colt[:, w % DEPTH, 3:4], colt[:, w % DEPTH, 3:4])
                    dve.drain()
                    V.tensor_scalar(pbuf[:, w % DEPTH, 0:u["nk"]], pbuf[:, w % DEPTH, 0:u["nk"]], colt[:, w % DEPTH, 3:4],
                                    scale_of(u), ALU.mult, ALU.mult if scale_of(u) is not None else ALU.bypass)\
                        .then_inc(u_pn[name], 1)

            dve.sem_inc(ada_free, 1)
            for k, s in rnd.items():
                dve.sem_inc(s, 3)
            dve.sem_inc(g_free, 4)
            dve.wait_ge(in_small, 16 * 13)
            for d in range(2):
                V.tensor_copy(dcol[64 * d:64 * d + 64, :, :], dall[64 * d:64 * d + 64, :, d::2])
            for k in range(2):
                V.tensor_tensor(flat(lamt[:, 2 * k:2 * k + 2, :]), lamv[:, 2 * k, :], lamv[:, 2 * k + 1, :], ALU.mult)
            dve.drain()
            V.tensor_reduce(small[:, 8:12], lamt[:, :, :], AX.X, ALU.add).then_inc(set_s, 1)
            dve.wait_ge(set_s, 2)
            V.tensor_tensor(small[:, 16:18], small[:, 14:16], small[:, 12:14], ALU.subtract)
            dve.wait_ge(set_e, 15)
            dve.drain()
            for l in range(2):
                init = 0.8 - 0.6 * math.exp(-0.3 * l)
                V.tensor_scalar(small[:, 20 + l:21 + l], small[:, 16 + l:17 + l], init, None, ALU.subtract)
                V.tensor_scalar(small[:, 24 + l:25 + l], prm(f"subln{l}"), 1.0 - init, None, ALU.mult)
            end(dve)

            begin(dve, "bias")
            dve.wait_ge(line_ps, 1)
            dve.wait_ge(in_w, 16 * 8)
            V.tensor_tensor(lines_b, PS[0][0:16, 0:LINE], lines_c, ALU.add).then_inc(line_sb, 1)
            dve.wait_ge(bias_in, 16)
            V.tensor_copy(biasT, biasraw[:, :, ::-1])
            end(dve)

            norm("norm1", S, lambda c, m: prm("norm1_g", k=c))

            def bias_table(head, u):
                return biasT[:, head, S - u["nk"]:S]

            begin(dve, "A")
            with rounds(dve, 4) as i:
                dve.wait_ge(rnd["A"], i * 3 + 3)
                ada("A", i)
                V.tensor_scalar(biasraw[:, 0:2, :], biasT[:, bass.ds(i * 2, 2), :], 1.0, None, ALU.mult)
                soft_all("A", i, Pb, cols, lambda u: biasraw[:, u["head"], S - u["nk"]:S], lambda u: None)
                dve.wait_ge(u_pv["A"], i * 4 + 4)
                V.tensor_scalar(mix1[:, bass.ds(i, 1), :], PS[3][:, 0:S].unsqueeze(1), 1.0, None, ALU.mult)
                dve.drain()
                dve.sem_inc(rnd["A"], 1)
            end(dve)

            begin(dve, "B")
            with rounds(dve, 2) as g:
                dve.wait_ge(rnd["B"], g * 3 + 3)
                V.tensor_scalar(biasraw[:, 0:4, :], biasT[:, bass.ds(g * 4 + 8, 4), :], 1.0, None, ALU.mult)
                made(dve, "B", 6, g)
                raw = PS[7][:, 0:S].rearrange("p (n l) -> p l n", l=16)
                for half in range(2):
                    last = V.tensor_tensor(blk[:, 16 * half:16 * half + 16, :], raw[:, :, half:half + 15],
                                           posT[:, 16 * half:16 * half + 16].unsqueeze(2).to_broadcast([P, 16, 15]), ALU.add)
                last.then_inc(bl_ready, 1)
                dve.wait_ge(kept["B"], g * 6 + 1)
                V.tensor_scalar(gsel[:, :, :], gate1[:, :, bass.ds(g * 12, 12)], 1.0, None, ALU.mult)
                dve.drain()
                soft_all("B", g, Pb, cols,
                         lambda u: (cst[:, C_CMP + 15 * u["qt"]:C_CMP + 15 * u["qt"] + 15] if u["branch"] == 0
                                    else biasraw[:, u["head"], S - u["nk"]:S]),
                         lambda u: gsel[:, u["qt"], 3 * u["head"] + u["branch"]:3 * u["head"] + u["branch"] + 1])
                dve.wait_ge(u_pv["B"], g * 24 + 24)
                V.tensor_scalar(mix1[:, bass.ds(g * 2 + 4, 2), :], PS[3][:, :].rearrange("p (c t) -> p c t", c=2),
                                1.0, None, ALU.mult)
                dve.drain()
                dve.sem_inc(rnd["B"], 1)
            end(dve)

            def last_slot(ph, n, t):
                own = len(loads[ph][1]) - (len(ADA[ph][1]) if ph in ADA else 0)
                return loads[ph][1][(t + 1) * own // n - 1][0]

            def residual(ph, times, n, n_tok, gate, l=0):
                begin(dve, ph)
                with rounds(dve, times) as i:
                    for t in range(n):
                        made(dve, ph, last_slot(ph, n, t), i)
                        for m, lo, hi in segments(n_tok):
                            h = hT[:, bass.ds(i * n + t, 1), lo:hi]
                            ps = PS[4 + t][:, lo:hi].unsqueeze(1)
                            if gate is None:
                                last = V.tensor_tensor(h, ps, h, ALU.add)
                            else:
                                last = V.scalar_tensor_tensor(out=h, in0=ps, scalar=modc[:, l, bass.ds(i * n + (gate + t), 1), m:m + 1]
                                                              .rearrange("p a b -> p (a b)"),
                                                              in1=h, op0=ALU.mult, op1=ALU.add)
                        last.then_inc(g_free, 1)
                    ada(ph, i)
                end(dve)

            residual("wout1", 2, 4, S, None)
            norm("norm2", S, lambda c, m: prm("norm2_g", k=c))
            begin(dve, "ffn1")
            with rounds(dve, FC1 // 2) as i:
                for n in range(2):
                    made(dve, "ffn1", 5 + 2 * n, i)
                    dve.wait_ge(g_mid, i * 2 + (n + 1))
                    V.tensor_tensor(hid1[:, bass.ds(i * 2 + n, 1), :], ffs[:, n, :].unsqueeze(1),
                                    PS[5 + 2 * n][:, 0:S].unsqueeze(1), ALU.mult).then_inc(g_free, 2)
            end(dve)
            residual("down1", 4, 2, S, None)
            norm("normf1", S, lambda c, m: prm("norm_f_g", k=c))

            mid = FC1
            for l in range(2):
                nt = wide(l)
                ph = f"ada{l}"
                begin(dve, ph)
                if l == 0:
                    V.tensor_copy(hT[:, :, 0:S], xnT[:, :, 0:S])
                dve.drain()
                for which, name in enumerate((f"mix{l}", f"mlp{l}")):
                    V.scalar_tensor_tensor(out=acol[:, which, :, :], in0=modc[:, l, 24 * which + 8:24 * which + 16, :],
                                           scalar=1.0, in1=prm(name, 8).unsqueeze(2).to_broadcast([P, 8, 2]),
                                           op0=ALU.add, op1=ALU.mult)
                end(dve)
                norm(f"mixnorm{l}", T, lambda c, m: acol[:, 0, c, m:m + 1])

                begin(dve, f"dt{l}")
                xb, ax, e, den, z, w2, tot, csr = dtw
                r = lambda t: t[0:64, :]
                dve.wait_ge(dt_pe, 6 * l + 1)
                V.tensor_scalar(r(xb), PS[4][0:64, :], small[0:64, l:l + 1], None, ALU.add)
                dve.drain()
                V.scalar_tensor_tensor(out=r(ax), in0=r(xb), scalar=-1.0, in1=r(xb), op0=ALU.mult, op1=ALU.max)\
                    .then_inc(dt_dve, 1)
                dve.wait_ge(dt_act, 5 * l + 1)
                V.tensor_scalar(r(den), r(e), 2.0, None, ALU.add)
                dve.drain()
                V.reciprocal(r(den), r(den))
                dve.drain()
                V.tensor_tensor(r(z), r(e), r(den), ALU.mult)
                dve.drain()
                V.tensor_tensor(r(w2), r(z), r(z), ALU.mult)
                dve.drain()
                V.tensor_scalar(r(e), r(w2), 1.0 / 17, None, ALU.mult)
                for k in (15, 13, 11, 9, 7, 5, 3):
                    dve.drain()
                    V.scalar_tensor_tensor(out=r(e), in0=r(e), scalar=1.0 / k, in1=r(w2), op0=ALU.add, op1=ALU.mult)
                dve.drain()
                V.scalar_tensor_tensor(out=r(e), in0=r(e), scalar=1.0, in1=r(z), op0=ALU.add, op1=ALU.mult)
                V.tensor_scalar(r(xb), r(xb), 0.0, None, ALU.max)
                dve.drain()
                V.scalar_tensor_tensor(out=r(xb), in0=r(e), scalar=2.0, in1=r(xb), op0=ALU.mult, op1=ALU.add)\
                    .then_inc(dt_dve, 1)
                dve.drain()
                V.tensor_scalar(r(ax), r(xb), small[0:64, 2 + l:3 + l], -1.0, ALU.mult, ALU.mult).then_inc(dt_dve, 1)
                dve.wait_ge(dt_pe, 6 * l + 4)
                V.tensor_copy(r(csr), PS[7][0:64, :]).then_inc(dt_dve, 4)
                dve.wait_ge(dt_pe, 6 * l + 5)
                V.tensor_scalar(tabs[:, 2, :, :], PS[0][:, 0:256].rearrange("p (c h) -> p c h", c=4), -1.0, None, ALU.mult)
                dve.wait_ge(dt_act, 5 * l + 4)
                dve.drain()
                V.tensor_tensor(tabs[:, 1, :, :], PS[3][:, 0:256].rearrange("p (c h) -> p c h", c=4), tabs[:, 2, :, :],
                                ALU.add).then_inc(dt_dve, 1)
                dve.wait_ge(dt_act, 5 * l + 5)
                V.tensor_tensor(tabs[:, 1, :, :], tabs[:, 1, :, :], tabs[:, 0, :, :], ALU.mult).then_inc(dt_dve, 1)
                dve.wait_ge(cs_out, 16 * (l + 1))
                end(dve)

                begin(dve, f"ssd{l}")
                n_ch = nt // P
                V.memset(ssq[:, :], 0.0)
                with rounds(dve, NG) as g:
                    R = lambda x, k, n: dve.wait_ge(ssd[l, x], g * k + n)
                    dve.wait_ge(rnd[f"ssd{l}"], g * 3 + 3)
                    V.memset(xpad[:, :, :, 0:2], 0.0)
                    V.memset(xpad[:, :, :, 258:260], 0.0)
                    for d in range(2):
                        V.tensor_copy(st4[:, :, d, :, :], tabs[:, :, :, bass.ds(g * 4 + 32 * d, 4)])
                    for t0, n, at in ((0, 2, g * 2), (2, 1, g + 16), (3, 1, g + 24)):
                        for q in range(2):
                            V.tensor_copy(cwc[:, t0:t0 + n, 3 * q:3 * q + 3].rearrange("p t k -> p k t"),
                                          prmT[:, 2 + 2 * l + q, 0:96].rearrange("p (k t) -> p k t", k=3)[:, :, bass.ds(at, n)])
                    V.tensor_copy(gd[:, 0, :], dcol[:, l, bass.ds(g * 2, 2)])
                    V.tensor_copy(gd[:, 1, :], prmT[:, 0, bass.ds(g * 2 + (64 + 16 * l), 2)])
                    ada(f"ssd{l}", g)
                    dve.drain()
                    for t in range(4):
                        R("padded", 4, t + 1)
                        acc = xs[:, t, :].rearrange("p (s n) -> p s n", s=2)
                        V.tensor_scalar(acc, xpad[:, t, :, 0:S], cwc[:, t, 0:1], None, ALU.mult)
                        for k in range(1, 5):
                            dve.drain()
                            last = V.scalar_tensor_tensor(out=acc, in0=xpad[:, t, :, k:k + S], scalar=cwc[:, t, k:k + 1],
                                                          in1=acc, op0=ALU.mult, op1=ALU.add)
                        last.then_inc(ssd[l, "conv"], 1)
                    R("tr", 2, 1)
                    for d in range(2):
                        for b in range(2):
                            V.tensor_tensor(xc[:, d, 2 * b:2 * b + 2, :].rearrange("p c (h e) -> p (c h) e", e=HD),
                                            PS[4 + b][:, :].rearrange("p (c e) -> p c e", e=HD),
                                            st4[:, 0, d, 2 * b:2 * b + 2, :].rearrange("p c h -> p (c h)").unsqueeze(2)
                                            .to_broadcast([P, 8, HD]), ALU.mult)
                    xcdv = xcd.rearrange("p d h c -> p d (h c)")
                    for step in range(3):
                        if step == 2:
                            R("states", 3, 1)
                        for d, order in enumerate((FWD, BWD)):
                            ch = order[step]
                            V.tensor_tensor(xcdv[:, d, (step % 2) * S:(step % 2) * S + S].rearrange("p (h e) -> p h e", e=HD),
                                            PS[4 + ch // 2][:, (ch % 2) * S:(ch % 2) * S + S].rearrange("p (h e) -> p h e", e=HD),
                                            st4[:, 1, d, ch, :].unsqueeze(2).to_broadcast([P, 4, HD]), ALU.mult)\
                                .then_inc(ssd[l, "xc"], 1)
                    R("tr", 2, 2)
                    for d, tri in enumerate((upper, lower)):
                        V.tensor_tensor(cbm[:, d, :, :], PS[7][:, :].rearrange("p (c t) -> p c t", c=4),
                                        tri.unsqueeze(1).to_broadcast([P, 4, P]), ALU.mult)
                    dve.drain()
                    dve.sem_inc(ssd[l, "cbm"], 1)
                    for step in range(3):
                        dve.drain()
                        R("states", 3, step + 1)
                        ps = PS[[2, 3, 2][step]]
                        if step == 0:
                            last = V.tensor_copy(H[:, :, 0, :], ps[:, :].rearrange("p (d c) -> p d c", d=2))
                        else:
                            for d, order in enumerate((FWD, BWD)):
                                for h in range(4):
                                    last = V.scalar_tensor_tensor(
                                        out=H[:, d, step, h * HD:(h + 1) * HD], in0=H[:, d, step - 1, h * HD:(h + 1) * HD],
                                        scalar=st4[:, 3, d, order[step], h:h + 1],
                                        in1=ps[:, d * S + h * HD:d * S + (h + 1) * HD], op0=ALU.mult, op1=ALU.add)
                        last.then_inc(ssd[l, "h"], 1)
                    R("ecs", 1, 1)
                    for d in range(2):
                        V.tensor_tensor(ecs[:, d, :, 0:nt], ecs[:, d, :, 0:nt],
                                        xs[:, 3, 0:nt].unsqueeze(1).to_broadcast([P, 4, nt]), ALU.mult)\
                            .then_inc(ssd[l, "cexp"], 1)
                    R("csb", 32, 32)
                    for ch in range(n_ch):
                        if ch:
                            R("ychunk", n_ch, ch)
                        for d in range(2):
                            for h in range(4):
                                last = V.tensor_scalar(mt[:, d, h, :], csb[:, d, h, ch * P:(ch + 1) * P],
                                                       st4[:, 2, d, ch, h:h + 1], 0.0, ALU.add, ALU.min)
                            last.then_inc(ssd[l, "mmin"], 1)
                        for d in range(2):
                            R("mexp", 2 * n_ch, 2 * ch + d + 1)
                            V.tensor_tensor(mt[:, d, :, :], mt[:, d, :, :],
                                            cbm[:, d, ch, :].unsqueeze(1).to_broadcast([P, 4, P]), ALU.mult)\
                                .then_inc(ssd[l, "mready"], 1)
                    R("ychunk", n_ch, n_ch)
                    for t in range(2):
                        V.scalar_tensor_tensor(out=y1[:, t, 0:nt], in0=xs[:, t, 0:nt], scalar=gd[:, 0, t:t + 1],
                                               in1=PS[4 + t][:, 0:nt], op0=ALU.mult, op1=ALU.add)
                    dve.drain()
                    R("gated", 2, 2)
                    for t in range(2):
                        V.tensor_tensor(y1[:, t, 0:nt], y1[:, t, 0:nt], zs[:, t, 0:nt], ALU.mult).then_inc(ssd[l, "y1"], 1)
                    dve.drain()
                    for t in range(2):
                        V.tensor_scalar(yz[:, bass.ds(g * 2 + t, 1), 0:nt], y1[:, t, 0:nt].unsqueeze(1), gd[:, 1, t:t + 1],
                                        None, ALU.mult)
                    R("ysum", 1, 1)
                    V.tensor_tensor(ssq[:, 0:nt], PS[2][:, 0:nt], ssq[:, 0:nt], ALU.add)
                    dve.drain()
                    dve.sem_inc(rnd[f"ssd{l}"], 1)
                V.tensor_scalar(ssq[:, 0:nt], ssq[:, 0:nt], 1.0 / DI, EPS, ALU.mult, ALU.add).then_inc(ssd_ms, 1)
                dve.wait_ge(ssd_rt, l + 1)
                V.reciprocal(ssq[:, 0:nt], ssq[:, 0:nt])
                end(dve)

                name = f"att{l}"
                begin(dve, name)
                with rounds(dve, 8) as h:
                    dve.wait_ge(rnd[name], h * 3 + 3)
                    ada(name, h)
                    dve.wait_ge(rot[name], h + 1)
                    cs = lambda c: cst[:, c:c + S].unsqueeze(1).to_broadcast([P, 2, S])
                    V.tensor_tensor(qkt[:, :, :], PS[7][:, :].rearrange("p (n t) -> p n t", n=2), cs(C_SIN), ALU.mult)
                    V.tensor_tensor(qk[:, :, 0:S], qk[:, :, 0:S], cs(C_COS), ALU.mult)
                    dve.drain()
                    V.tensor_tensor(qk[:, :, 0:S], qk[:, :, 0:S], qkt[:, :, :], ALU.add).then_inc(roped[name], 1)
                    soft_all(name, h, Pa, cola, None, lambda u: small[:, 20 + l:21 + l] if u["comp"] else None)
                    nu = len(units[name])
                    dve.wait_ge(u_pv[name], h * nu + nu)
                    V.tensor_scalar(attT[:, bass.ds(h, 1), 0:nt], PS[3][:, 0:nt].unsqueeze(1), 1.0, None, ALU.mult)
                    dve.drain()
                    dve.sem_inc(rnd[name], 1)
                for h in range(8):
                    dve.wait_ge(sub_p, 8 * l + h + 1)
                    dve.drain()
                    V.tensor_scalar(osb[:, 0:nt], PS[0][:, 0:nt], 1.0 / P, EPS, ALU.mult, ALU.add).then_inc(sub_r, 1)
                    dve.wait_ge(sub_r, 16 * l + 2 * h + 2)
                    V.reciprocal(osb[:, 0:nt], osb[:, 0:nt])
                    dve.drain()
                    V.scalar_tensor_tensor(out=attT[:, h, 0:nt], in0=attT[:, h, 0:nt], scalar=small[:, 24 + l:25 + l],
                                           in1=osb[:, 0:nt], op0=ALU.mult, op1=ALU.mult)
                end(dve)

                ph = f"merge{l}"
                begin(dve, ph)
                with rounds(dve, 8) as i:
                    dve.wait_ge(g_mid, i * 2 + (mid + 2))
                    made(dve, ph, 2, i)
                    V.tensor_tensor(fr[:, 1, 0:nt], fr[:, 1, 0:nt], ssq[:, 0:nt], ALU.mult)
                    V.tensor_tensor(fr[:, 0, 0:nt], fr[:, 0, 0:nt], PS[6][:, 0:nt], ALU.mult)
                    dve.drain()
                    V.tensor_tensor(fr[:, 1, 0:nt], fr[:, 1, 0:nt], PS[7][:, 0:nt], ALU.mult)
                    dve.drain()
                    V.tensor_tensor(mT[:, bass.ds(i, 1), 0:nt], fr[:, 0, 0:nt].unsqueeze(1), fr[:, 1, 0:nt].unsqueeze(1),
                                    ALU.add)
                    dve.drain()
                    dve.sem_inc(g_free, 4)
                mid += 16
                end(dve)
                residual(f"wout2{l}", 2, 4, nt, 16, l)
                norm(f"mlpnorm{l}", nt, lambda c, m: acol[:, 1, c, m:m + 1])
                begin(dve, f"f1{l}")
                with rounds(dve, 8) as i:
                    for n in range(4):
                        dve.wait_ge(g_mid, i * 4 + (mid + n + 1))
                        f = fr[:, n, 0:nt].unsqueeze(1)
                        V.tensor_tensor(hid2[:, bass.ds(i * 4 + n, 1), 0:nt], f, f, ALU.mult).then_inc(g_free, 1)
                mid += 32
                end(dve)
                residual(f"f2{l}", 4, 2, nt, 40, l)
            norm("normend", S, lambda c, m: prm("final", k=c))
            begin(dve, "out")
            end(dve)


NAMES = [
    "x", "norm1_g", "w_in", "rel_bias", "cmp_pos", "cmp_k_w1", "cmp_k_b1", "cmp_k_w2", "cmp_v_w1", "cmp_v_b1",
    "cmp_v_w2", "w_out", "norm2_g", "w_gate", "w_up", "w_down", "norm_f_g", "c_2", "ctx_2", "c_ctx_2", "ada_w_2",
    "ada_b_2", "norm_mix_g_2", "w_in_2", "conv_w_2", "conv_b_2", "dt_bias_f_2", "dt_bias_b_2", "a_log_f_2",
    "a_log_b_2", "ssd_d_2", "ssd_norm_g_2", "lambda_q1_2", "lambda_k1_2", "lambda_q2_2", "lambda_k2_2",
    "attn_subln_g_2", "w_attn_o_2", "w_ssd_o_2", "w_out_2", "norm_mlp_g_2", "w_mlp1_2", "w_mlp2_2", "final_norm_g_2",
]


def kernel(**inputs):
    import concourse.bacc as bacc
    from concourse.bass_utils import run_bass_kernel_spmd

    nc = bacc.Bacc("TRN2", target_bir_lowering=False, num_devices=1)
    arrays, aps = {}, {}
    for name, value in [(n, np.ascontiguousarray(inputs[n])) for n in NAMES] + list(constants().items()):
        arrays[f"in_{name}"] = value
        aps[name] = nc.dram_tensor(f"in_{name}", value.shape, mybir.dt.from_np(value.dtype), kind="ExternalInput").ap()
    out = nc.dram_tensor("out_0", (1, S, D), mybir.dt.float32, kind="ExternalOutput").ap()
    build(nc, aps, out)
    r = run_bass_kernel_spmd(nc, [arrays], core_ids=[0])
    return r.results[0]["out_0"]
```
